# Optimizing a Trainium2 kernel written in Bass

```python
import jax, jax.numpy as jnp
from jax import lax
import numpy as np

D_MODEL = 1024
BATCH = 1
SEQ = 512
DEPTH = 1

HEAD_DIM = 64
ROPE_THETA = 10000.0
EPS = 1e-6
SWA_Q_HEADS = 8
SWA_KV_HEADS = 2
SWA_WINDOW = 128
SWA_BLOCK = 128
MOBA_HEADS = 8
MOBA_BLOCK = 256
MOBA_TOPK = 3
MOBA_Q_CHUNK = 16
GLA_HEADS = 4
GLA_DK = 64
GLA_DV = 128
GLA_GATE_RANK = 16
GLA_TAU = 16.0
GLA_CHUNK = 64
N_BRANCH = 3
SWA_WIDTH = SWA_Q_HEADS * HEAD_DIM
MOBA_WIDTH = MOBA_HEADS * HEAD_DIM
GLA_WIDTH = GLA_HEADS * GLA_DV
D_FF = -(-8 * D_MODEL // (3 * 256)) * 256
IN_SIZES = (
    SWA_Q_HEADS * HEAD_DIM, SWA_KV_HEADS * HEAD_DIM, SWA_KV_HEADS * HEAD_DIM,
    MOBA_HEADS * HEAD_DIM, MOBA_HEADS * HEAD_DIM, MOBA_HEADS * HEAD_DIM,
    GLA_HEADS * GLA_DK, GLA_HEADS * GLA_DK, GLA_HEADS * GLA_DV,
    GLA_GATE_RANK, GLA_HEADS * GLA_DV,
    N_BRANCH * D_MODEL,
)
D_IN = sum(IN_SIZES)

kernel_name = "hybrid_swa_moba_gla_block"

def rms_norm(x, g):
    xf = x.astype(jnp.float32)
    y = xf * lax.rsqrt(jnp.mean(xf * xf, axis=-1, keepdims=True) + EPS)
    return (y * g.astype(jnp.float32)).astype(x.dtype)

def rope_tables(positions, dim, dtype):
    inv_freq = ROPE_THETA ** (-jnp.arange(0, dim, 2, dtype=jnp.float32) / dim)
    ang = positions.astype(jnp.float32)[..., None] * inv_freq
    return jnp.cos(ang)[:, :, None, :].astype(dtype), jnp.sin(ang)[:, :, None, :].astype(dtype)

def apply_rope(x, cos, sin):
    x1, x2 = jnp.split(x, 2, axis=-1)
    return jnp.concatenate([x1 * cos - x2 * sin, x2 * cos + x1 * sin], axis=-1)

def sliding_window_attention(q, k, v, sinks):
    B, S, Hq, d = q.shape
    Hkv = k.shape[2]
    G = Hq // Hkv
    L = SWA_BLOCK
    nb = S // L
    qb = q.reshape(B, nb, L, Hkv, G, d)
    pad = lambda t: jnp.pad(t, ((0, 0), (L, 0), (0, 0), (0, 0))).reshape(B, nb + 1, L, Hkv, d)
    kp, vp = pad(k), pad(v)
    kb = jnp.concatenate([kp[:, :-1], kp[:, 1:]], axis=2)
    vb = jnp.concatenate([vp[:, :-1], vp[:, 1:]], axis=2)
    s = jnp.einsum('bnqhgd,bnkhd->bnhgqk', qb, kb).astype(jnp.float32) * (d ** -0.5)
    qi = jnp.arange(L)[:, None]
    ki = jnp.arange(2 * L)[None, :]
    rel = qi + L - ki
    kpos = jnp.arange(nb)[:, None, None] * L + ki - L
    allowed = (rel >= 0) & (rel < SWA_WINDOW) & (kpos >= 0)
    s = jnp.where(allowed[None, :, None, None], s, -jnp.inf)
    sink = sinks.astype(jnp.float32).reshape(1, 1, Hkv, G, 1, 1)
    m = jnp.maximum(jnp.max(s, axis=-1, keepdims=True), sink)
    p = jnp.exp(s - m)
    p = (p / (jnp.sum(p, axis=-1, keepdims=True) + jnp.exp(sink - m))).astype(v.dtype)
    o = jnp.einsum('bnhgqk,bnkhd->bnqhgd', p, vb)
    return o.reshape(B, S, Hq * d)

def moba_attention(q, k, v):
    B, S, H, d = q.shape
    L = MOBA_BLOCK
    nb = -(-S // L)
    Sp = nb * L
    scale = d ** -0.5
    padS = lambda t: jnp.pad(t, ((0, 0), (0, Sp - S), (0, 0), (0, 0))).transpose(0, 2, 1, 3)
    qh, kh, vh = padS(q), padS(k), padS(v)
    kblk = kh.reshape(B, H, nb, L, d)
    vblk = vh.reshape(B, H, nb, L, d)
    kmean = jnp.mean(kblk.astype(jnp.float32), axis=3)
    gate = jnp.einsum('bhtd,bhnd->bhtn', qh.astype(jnp.float32), kmean)
    past = jnp.arange(nb)[None, :] < (jnp.arange(Sp) // L)[:, None]
    gate = jnp.where(past, gate, -jnp.inf)
    topk = min(MOBA_TOPK, nb)
    gval, gidx = lax.top_k(gate, topk)
    gvalid = jnp.isfinite(gval)

    C = MOBA_Q_CHUNK
    nc = Sp // C
    to_chunks = lambda t: jnp.moveaxis(t.reshape(B, H, nc, C, t.shape[-1]), 2, 0)
    bi = jnp.arange(B)[:, None, None, None]
    hi = jnp.arange(H)[None, :, None, None]

    def one_chunk(args):
        qc, ic, vc_ok, c = args
        ksel = kblk[bi, hi, ic]
        vsel = vblk[bi, hi, ic]
        s_sel = jnp.einsum('bhqd,bhqnkd->bhqnk', qc, ksel).astype(jnp.float32) * scale
        s_sel = jnp.where(vc_ok[..., None], s_sel, -jnp.inf).reshape(B, H, C, topk * L)
        own = (c * C) // L
        kown = lax.dynamic_index_in_dim(kblk, own, axis=2, keepdims=False)
        vown = lax.dynamic_index_in_dim(vblk, own, axis=2, keepdims=False)
        s_own = jnp.einsum('bhqd,bhkd->bhqk', qc, kown).astype(jnp.float32) * scale
        qpos = c * C + jnp.arange(C)
        kpos = own * L + jnp.arange(L)
        s_own = jnp.where(kpos[None, :] <= qpos[:, None], s_own, -jnp.inf)
        p = jax.nn.softmax(jnp.concatenate([s_sel, s_own], axis=-1), axis=-1).astype(vh.dtype)
        p_sel = p[..., :topk * L].reshape(B, H, C, topk, L)
        p_own = p[..., topk * L:]
        return (jnp.einsum('bhqnk,bhqnkd->bhqd', p_sel, vsel)
                + jnp.einsum('bhqk,bhkd->bhqd', p_own, vown))

    out = lax.map(one_chunk, (to_chunks(qh), to_chunks(gidx), to_chunks(gvalid),
                              jnp.arange(nc, dtype=jnp.int32)))
    out = jnp.moveaxis(out, 0, 2).reshape(B, H, Sp, d)[:, :, :S]
    return out.transpose(0, 2, 1, 3).reshape(B, S, H * d)

def gla_attention(q, k, v, log_alpha):
    B, S, H, dk = q.shape
    dv = v.shape[-1]
    C = GLA_CHUNK
    nc = S // C
    f32 = jnp.float32
    rs = lambda t: t.astype(f32).reshape(B, nc, C, H, t.shape[-1]).transpose(0, 3, 1, 2, 4)
    qc = rs(q) * (dk ** -0.5)
    kc, vc = rs(k), rs(v)
    b = jnp.cumsum(rs(log_alpha), axis=3)
    b_last = b[..., -1:, :]
    q_dec = qc * jnp.exp(b)
    k_dec = kc * jnp.exp(-b)
    k_tail = kc * jnp.exp(b_last - b)
    A = jnp.einsum('bhnid,bhnjd->bhnij', q_dec, k_dec)
    A = jnp.where(jnp.tril(jnp.ones((C, C), dtype=bool)), A, 0.0)
    o_intra = jnp.einsum('bhnij,bhnjv->bhniv', A, vc)
    dS = jnp.einsum('bhnjd,bhnjv->bhndv', k_tail, vc)
    decay = jnp.exp(b_last[..., 0, :])

    def step(state, inp):
        dec, ds = inp
        return dec[..., None] * state + ds, state

    _, s_before = lax.scan(step, jnp.zeros((B, H, dk, dv), f32),
                           (jnp.moveaxis(decay, 2, 0), jnp.moveaxis(dS, 2, 0)))
    o_inter = jnp.einsum('bhnid,bhndv->bhniv', q_dec, jnp.moveaxis(s_before, 0, 2))
    o = o_intra + o_inter
    return o.transpose(0, 2, 3, 1, 4).reshape(B, S, H, dv).astype(v.dtype)

def hybrid_mixer(h, cos, sin, w_in, swa_q_norm, swa_k_norm, swa_sinks, moba_q_norm, moba_k_norm,
                 gla_w_alpha, gla_b_alpha, gla_out_norm, w_branch_swa, w_branch_moba, w_branch_gla, w_out):
    B, S, D = h.shape
    proj = h @ w_in
    points = np.cumsum(IN_SIZES)[:-1].tolist()
    (qa, ka, va, qb, kb, vb, qg, kg, vg, a_low, r_gate, gates) = jnp.split(proj, points, axis=-1)
    heads = lambda t, n: t.reshape(B, S, n, -1)
    qa = apply_rope(rms_norm(heads(qa, SWA_Q_HEADS), swa_q_norm), cos, sin)
    ka = apply_rope(rms_norm(heads(ka, SWA_KV_HEADS), swa_k_norm), cos, sin)
    y_a = sliding_window_attention(qa, ka, heads(va, SWA_KV_HEADS), swa_sinks)
    qb = apply_rope(rms_norm(heads(qb, MOBA_HEADS), moba_q_norm), cos, sin)
    kb = apply_rope(rms_norm(heads(kb, MOBA_HEADS), moba_k_norm), cos, sin)
    y_b = moba_attention(qb, kb, heads(vb, MOBA_HEADS))
    log_alpha = jax.nn.log_sigmoid((a_low @ gla_w_alpha + gla_b_alpha).astype(jnp.float32)) / GLA_TAU
    o_c = gla_attention(heads(qg, GLA_HEADS), heads(kg, GLA_HEADS), heads(vg, GLA_HEADS),
                        log_alpha.reshape(B, S, GLA_HEADS, GLA_DK))
    y_c = rms_norm(o_c, gla_out_norm).reshape(B, S, GLA_WIDTH) * jax.nn.silu(r_gate)
    g = jax.nn.sigmoid(gates.reshape(B, S, N_BRANCH, D))
    merged = (g[:, :, 0] * (y_a @ w_branch_swa)
              + g[:, :, 1] * (y_b @ w_branch_moba)
              + g[:, :, 2] * (y_c @ w_branch_gla))
    return merged @ w_out

def swiglu(h, w_gate, w_up, w_down):
    return (jax.nn.silu(h @ w_gate) * (h @ w_up)) @ w_down

def setup_inputs(seed: int = 0) -> dict:
    key = jax.random.key(seed)
    ks = jax.random.split(key, 24)
    f32 = jnp.float32
    nrm = lambda k, shape, scale: jax.random.normal(k, shape, f32) * scale
    gain = lambda k, shape: 1.0 + 0.05 * jax.random.normal(k, shape, f32)
    return {
        "x": nrm(ks[0], (BATCH, SEQ, D_MODEL), 1.0),
        "positions": jnp.broadcast_to(jnp.arange(SEQ, dtype=jnp.int32), (BATCH, SEQ)),
        "attn_norm": gain(ks[1], (DEPTH, D_MODEL)),
        "w_in": nrm(ks[2], (DEPTH, D_MODEL, D_IN), D_MODEL ** -0.5),
        "swa_q_norm": gain(ks[3], (DEPTH, HEAD_DIM)),
        "swa_k_norm": gain(ks[4], (DEPTH, HEAD_DIM)),
        "swa_sinks": nrm(ks[5], (DEPTH, SWA_Q_HEADS), 0.5),
        "moba_q_norm": gain(ks[6], (DEPTH, HEAD_DIM)),
        "moba_k_norm": gain(ks[7], (DEPTH, HEAD_DIM)),
        "gla_w_alpha": nrm(ks[8], (DEPTH, GLA_GATE_RANK, GLA_HEADS * GLA_DK), GLA_GATE_RANK ** -0.5),
        "gla_b_alpha": nrm(ks[9], (DEPTH, GLA_HEADS * GLA_DK), 0.1),
        "gla_out_norm": gain(ks[10], (DEPTH, GLA_DV)),
        "w_branch_swa": nrm(ks[11], (DEPTH, SWA_WIDTH, D_MODEL), SWA_WIDTH ** -0.5),
        "w_branch_moba": nrm(ks[12], (DEPTH, MOBA_WIDTH, D_MODEL), MOBA_WIDTH ** -0.5),
        "w_branch_gla": nrm(ks[13], (DEPTH, GLA_WIDTH, D_MODEL), GLA_WIDTH ** -0.5),
        "w_out": nrm(ks[14], (DEPTH, D_MODEL, D_MODEL), D_MODEL ** -0.5),
        "ffn_norm": gain(ks[15], (DEPTH, D_MODEL)),
        "w_ffn_gate": nrm(ks[16], (DEPTH, D_MODEL, D_FF), D_MODEL ** -0.5),
        "w_ffn_up": nrm(ks[17], (DEPTH, D_MODEL, D_FF), D_MODEL ** -0.5),
        "w_ffn_down": nrm(ks[18], (DEPTH, D_FF, D_MODEL), D_FF ** -0.5),
    }

def reference(x, positions, attn_norm, w_in, swa_q_norm, swa_k_norm, swa_sinks, moba_q_norm, moba_k_norm,
              gla_w_alpha, gla_b_alpha, gla_out_norm, w_branch_swa, w_branch_moba, w_branch_gla, w_out,
              ffn_norm, w_ffn_gate, w_ffn_up, w_ffn_down):
    cos, sin = rope_tables(positions, HEAD_DIM, x.dtype)
    for l in range(DEPTH):
        h = rms_norm(x, attn_norm[l])
        x = x + hybrid_mixer(h, cos, sin, w_in[l], swa_q_norm[l], swa_k_norm[l], swa_sinks[l],
                             moba_q_norm[l], moba_k_norm[l], gla_w_alpha[l], gla_b_alpha[l],
                             gla_out_norm[l], w_branch_swa[l], w_branch_moba[l], w_branch_gla[l], w_out[l])
        h = rms_norm(x, ffn_norm[l])
        x = x + swiglu(h, w_ffn_gate[l], w_ffn_up[l], w_ffn_down[l])
    return x


_drawn_inputs = setup_inputs


def setup_inputs(seed=0):
    import zlib

    import numpy as np

    out = dict(_drawn_inputs(seed))
    spreads = {}
    factors = {'swa_q_norm': 8.0,
     'swa_k_norm': 8.0,
     'swa_sinks': 200.0,
     'moba_q_norm': 8.0,
     'moba_k_norm': 8.0,
     'gla_b_alpha': 3.664,
     'gla_out_norm': 2.91}
    for name, (base, spread) in spreads.items():
        noise = np.random.default_rng([zlib.crc32(name.encode()), seed]).standard_normal(out[name].shape)
        drawn = base * np.exp(spread * noise) if base else spread * noise
        out[name] = __import__('jax').numpy.asarray(drawn.astype(out[name].dtype))
    for name, factor in factors.items():
        out[name] = (out[name] * factor).astype(out[name].dtype)
    return out
```

```python
from contextlib import ExitStack

import numpy as np

import concourse.bass as bass
from concourse import mybir

F32 = mybir.dt.float32
F32R = mybir.dt.float32r
BF16 = mybir.dt.bfloat16
I32 = mybir.dt.int32
ALU = mybir.AluOpType
ACT = mybir.ActivationFunctionType
AX_X = mybir.AxisListType.X

P = 128
D = 1024
S = 512
T = S // P
K = D // P
HD = 64
HEADS = 8
KV = 2
GPK = HEADS // KV
WINDOW = 128
BW = 512
BR = BW // P
GH, GDK, GDV, GC = 4, 64, 128, 64
NCH = S // GC
RANK = 16
F = 2816
FK = F // P
EPS = 1e-6
NEG = -1e30

C_QA, C_KA, C_VA, C_QB, C_KB, C_VB = 0, 512, 640, 768, 1280, 1792
C_QG, C_VG, C_VG2, C_R, C_GATE = 2304, 2816, 3072, 3344, 3856
NA = C_QG
LOW = 512
NV = LOW + RANK

ST_G = K - 1 + 4
ST_GATE0 = 8 * ST_G
ST_HEAD = 2 + K - 1 + 1
ST_BR0 = ST_GATE0 + HEADS * ST_HEAD
ST_BR = 12
ST_O0 = ST_BR0 + 4 * ST_BR
ST_F0 = ST_O0 + 2 * ST_G
FG = F // 256
ST_D0 = ST_F0 + FG * ST_G
ST_D = FK - 1 + T
RING = K
DRING = 11
LD_G = 16 * 8
LD_O = LD_G + 48 * 12
LD_F = LD_O + 16 * 2
LD_D = LD_F + 32 * FG


def build_layer(nc, x, positions, attn_norm, w_in, swa_q_norm, swa_k_norm, swa_sinks, moba_q_norm,
                moba_k_norm, gla_w_alpha, gla_b_alpha, gla_out_norm, w_branch_swa, w_branch_moba,
                w_branch_gla, w_out, ffn_norm, w_ffn_gate, w_ffn_up, w_ffn_down, out):
    ctx = ExitStack()
    with ctx:
        def sem(name):
            return ctx.enter_context(nc.semaphore(name))

        base = 16512
        R_RING = base
        R_H = R_RING + 3 * RING * 2048
        R_NAT = R_H + 2 * K * 2048
        R_NATV = R_NAT + T * NA * 4
        R_GT = R_NATV + T * NV * 4
        R_WORK = R_GT + HEADS * 3 * 2048
        R_CONST = R_WORK + 16 * 2048

        def at(name, shape, dt, offset):
            return nc.alloc_sbuf_tensor_at(name, shape, dt, offset=offset)

        raw = [at(f"raw{s}", [P, 512], F32, R_RING + s * 2048) for s in range(RING)]
        whi = [at(f"whi{s}", [P, 512], F32R, R_RING + (RING + s) * 2048) for s in range(RING)]
        wlo = [at(f"wlo{s}", [P, 512], F32R, R_RING + (2 * RING + s) * 2048) for s in range(RING)]
        hT_h = at("hT_h", [P, K, S], F32R, R_H)
        hT_l = at("hT_l", [P, K, S], F32R, R_H + K * 2048)
        ya_h = at("ya_h", [P, 2 * BR, S], F32R, R_H)
        ya_l = at("ya_l", [P, 2 * BR, S], F32R, R_H + K * 2048)
        fT_h = at("fT_h", [P, K, S], F32R, R_H)
        fT_l = at("fT_l", [P, K, S], F32R, R_H + K * 2048)
        for s in range(RING, DRING):
            raw.append(at(f"raw{s}", [P, 512], F32, R_H + (s - RING) * 2048))
            whi.append(at(f"whi{s}", [P, 512], F32R, R_H + (3 + s - RING) * 2048))
            wlo.append(at(f"wlo{s}", [P, 512], F32R, R_H + (6 + s - RING) * 2048))
        nat = at("nat", [P, T, NA], F32, R_NAT)
        natv = at("natv", [P, T, NV], F32, R_NATV)
        mT_h = at("mT_h", [P, K, S], F32R, R_NAT)
        mT_l = at("mT_l", [P, K, S], F32R, R_NAT + K * 2048)
        aT_h = at("aT_h", [P, FK, S], F32R, R_NAT)
        aT_l = at("aT_l", [P, FK, S], F32R, R_NAT + FK * 2048)
        ycT = at("ycT", [P, BR, S], F32, R_NATV)
        mtmp = at("mtmp", [P, 4, S], F32, R_NATV)
        tg = at("tg", [P, HEADS, 3, S], F32, R_GT)
        qk = at("qk", [P, 4, S], F32, R_GT)
        lab = at("lab", [P, 2, S], F32, R_GT + 8192)
        gx = at("gx", [P, 2, S], F32, R_GT + 12288)
        kt = at("kt", [P, 2, S], F32, R_GT + 16384)
        ktn = at("ktn", [P, T, 2 * P], F32, R_GT + 20480)
        st = at("st", [P, 2, NCH, GDV], F32, R_GT + 24576)
        am = at("am", [P, T, 2, 2, P], F32, R_GT + 32768)
        srT = at("srT", [P, BR, S], F32, R_GT + 40960)
        alT = at("alT", [RANK, S], F32, R_GT + 40960)
        once = at("once", [P, S], F32, R_GT + 43008)
        osq = at("osq", [P, T, S], F32, R_GT + 12288)
        ang = at("ang", [P, 6, T, HD // 2], F32, R_GT + 16384)
        cmask = at("cmask", [P, P], I32, R_GT + 45056)
        vecs = at("vecs", [19, P], F32, R_GT)
        cm = at("cm", [P, P], F32, R_NATV)
        posi = at("posi", [T, P], I32, R_GT + 512)
        posf = at("posf", [T, P], F32, R_GT + 1024)
        invf = at("invf", [P, HD // 2], F32, R_GT + 19456)
        gain = at("gain", [P, 4, HD], F32, R_GT + 20480)
        wal = at("wal", [RANK, GH * GDK], F32, R_GT + 21504)
        X0 = at("X0", [P, T, D], F32, R_WORK + 16384)
        sqx = at("sqx", [P, D], F32, R_WORK)
        diag = at("diag", [P, T, P], F32, R_WORK + 8192)
        ctab = at("ctab", [P, 4, T, HD], F32, R_WORK)
        stab = at("stab", [P, 4, T, HD], F32, R_WORK + 4096)
        ropa = at("ropa", [P, T, HEADS, HD], F32, R_WORK + 8192)
        ropb = at("ropb", [P, T, HEADS, HD], F32, R_WORK + 16384)
        sqr = at("sqr", [P, T, HEADS, HD], F32, R_WORK + 24576)
        NP_M, NP_S = T * (T + 1) // 2, 2 * T - 1
        pr = at("pr", [P, (NP_M + NP_S) * P], F32, R_WORK)
        prT = at("prT", [P, NP_M + NP_S, P], F32, R_WORK + 8704)
        stg = at("stg", [P, T, 2, 2, HD], F32, R_WORK + 17408)
        qkT = at("qkT", [P, 2, S], F32, R_WORK + 21504)
        yc_h = at("yc_h", [P, BR, S], F32R, R_WORK)
        yc_l = at("yc_l", [P, BR, S], F32R, R_WORK + 8192)
        X = at("X", [P, T, D], F32, R_WORK + 16384)
        fa = at("fa", [P, 8, S], F32, R_WORK)
        off = [R_CONST]

        def small(name, shape, dt):
            n = 1
            for v in shape[1:]:
                n *= v
            t = at(name, shape, dt, off[0])
            off[0] += -(-n * (2 if dt == BF16 else 4) // 32) * 32
            return t

        ident = small("ident", [P, P], F32)
        identb = small("identb", [P, P], BF16)
        wmask = small("wmask", [P, 2 * P], BF16)
        vT = small("vT", [P, 19], F32)
        pT = small("pT", [P, T], F32)
        sinks = small("sinks", [P, HEADS], F32)
        nsinks = small("nsinks", [P, HEADS], F32)
        ss = small("ss", [P, 32], F32)
        rv = small("rv", [P, 32], F32)
        ry = small("ry", [P, 32], F32)
        ru = small("ru", [P, 32], F32)
        mx = small("mx", [P, 8], F32)
        den = small("den", [P, 8], F32)
        esk = small("esk", [P, 4], F32)
        rec = small("rec", [P, 8], F32)
        dec = small("dec", [P, 2, NCH], F32)
        assert off[0] <= 229344, off[0]

        PS = ctx.enter_context(nc.psum_tensor("PS", [P, 8, 512], F32))

        x_landed = [sem(f"x_landed{t}") for t in range(T)]
        vec_landed = sem("vec_landed")
        small_landed = sem("small_landed")
        x_again = sem("x_again")
        w_landed = [sem(f"w_landed{s}") for s in range(DRING)]
        out_landed = sem("out_landed")
        consts = sem("consts")
        am_zero = sem("am_zero")
        lo_done = sem("lo_done")
        hi_done = sem("hi_done")
        w_steps = sem("w_steps")
        act_seq = sem("act_seq")
        dve_seq = sem("dve_seq")
        acc_free = sem("acc_free")
        vec_T = sem("vec_T")
        vec_ready = sem("vec_ready")
        x_squared = sem("x_squared")
        diag_ready = sem("diag_ready")
        x_T = sem("x_T")
        hT_hi = sem("hT_hi")
        hT_done = sem("hT_done")
        ang_ready = sem("ang_ready")
        sin_done = sem("sin_done")
        low_T = sem("low_T")
        low_ready = sem("low_ready")
        z_done = sem("z_done")
        z_read = sem("z_read")
        soft_done = sem("soft_done")
        b_ready = sem("b_ready")
        gexp = sem("gexp")
        gexp_used = sem("gexp_used")
        kt_T = sem("kt_T")
        kt_ready = sem("kt_ready")
        a_done = sem("a_done")
        a_ready = sem("a_ready")
        ds_done = sem("ds_done")
        st_ready = sem("st_ready")
        o_half = sem("o_half")
        o_done = sem("o_done")
        o_copied = sem("o_copied")
        o_squared = sem("o_squared")
        o_normed = sem("o_normed")
        yc_T = sem("yc_T")
        yc_done = sem("yc_done")
        r_tanh = sem("r_tanh")
        rope_sq = sem("rope_sq")
        sqr_read = sem("sqr_read")
        rope_done = sem("rope_done")
        staged = sem("staged")
        kstaged = sem("kstaged")
        qk_T = sem("qk_T")
        qkT_ready = sem("qkT_ready")
        scores = sem("scores")
        negmax = sem("negmax")
        probs = sem("probs")
        pr_T = sem("pr_T")
        prT_v = sem("prT_v")
        prT_a = sem("prT_a")
        pv = sem("pv")
        y_ready = sem("y_ready")
        gate_read = sem("gate_read")
        y_T = sem("y_T")
        y_hi = sem("y_hi")
        y_lo = sem("y_lo")
        merge_read = sem("merge_read")
        merged = sem("merged")
        m_hi = sem("m_hi")
        m_lo = sem("m_lo")
        x2_ready = sem("x2_ready")
        f_tanh = sem("f_tanh")
        f_mid = sem("f_mid")
        f_read = sem("f_read")
        f_hi = sem("f_hi")
        f_lo = sem("f_lo")
        y_out = sem("y_out")

        block = ctx.enter_context(nc.Block())

        def rows(w, k):
            return w[k * P:(k + 1) * P]

        QUAD = 4 * HD
        CHUNKS = [[(C_QA, HEADS, 0)], [(C_KA, KV, 1), (C_QB, 4, 2)],
                  [(C_QB + QUAD, 4, 2), (C_KB, 4, 3)], [(C_KB + QUAD, 4, 3)]]

        Y_ORDER = (4, 5, 6, 1, 0, 2, 3, 7)
        Y_BANK = (3, 4, 5, 6, 7, 1, 0, 3)
        B_ORDER = (2, 1, 0)
        R_ORDER = (0, 3, 1, 2)

        M_AT = {3: (3, 0), 2: (4, 0), 0: (4, 384), 1: (5, 0)}
        S_AT = {1: (6, 0), 2: (6, 256), 3: (7, 0), 0: (7, 256)}
        M_PR = [t * (t + 1) // 2 for t in range(T)]
        S_PR = [NP_M + max(0, 2 * t - 1) for t in range(T)]
        NPR = NP_M + NP_S

        @block.sync
        def _(sp):
            def load(s, dst, src):
                sp.dma_start(dst, src).then_inc(w_landed[s], 16)

            def raw_free(k, group):
                sp.wait_ge(lo_done, K * (group - 1) + k + 1)

            for t in range(T):
                sp.dma_start(X0[:, t, :], x[0, t * P:(t + 1) * P, :]).then_inc(x_landed[t], 16)
            for dst, src in ((vecs[0:K, :], attn_norm.rearrange("a (k p) -> (a k) p", p=P)),
                             (vecs[K:2 * K, :], ffn_norm.rearrange("a (k p) -> (a k) p", p=P)),
                             (vecs[16:18, :], gla_b_alpha.rearrange("a (k p) -> (a k) p", p=P)),
                             (vecs[18:19, :], gla_out_norm),
                             (posi[:, :], positions.rearrange("a (k p) -> (a k) p", p=P))):
                sp.dma_start(dst, src).then_inc(vec_landed, 16)
            for k in range(K):
                load(k, raw[k][:, :], rows(w_in, k)[:, C_QG:C_QG + 512])
            for dst, src in ((gain[:, 0, :], swa_q_norm.to_broadcast([P, HD])),
                             (gain[:, 1, :], swa_k_norm.to_broadcast([P, HD])),
                             (gain[:, 2, :], moba_q_norm.to_broadcast([P, HD])),
                             (gain[:, 3, :], moba_k_norm.to_broadcast([P, HD])),
                             (sinks[:, :], swa_sinks.to_broadcast([P, HEADS])),
                             (wal[:, :], gla_w_alpha[0])):
                sp.dma_start(dst, src).then_inc(small_landed, 16)
            for k in range(K):
                raw_free(k, 1)
                load(k, raw[k][:, 0:272], rows(w_in, k)[:, C_VG2:C_VG2 + 272])
            for k in range(K):
                raw_free(k, 2)
                two = rows(w_in, k)[:, C_QG - 256:C_VG + 256]
                src = bass.AP(two.tensor, two.offset, [list(two.ap[0]), [C_VG - C_QG + 256, 2], [1, 256]])
                load(k, raw[k][:, :].rearrange("p (a n) -> p a n", a=2), src)
            with sp.Fori(3, 7) as g:
                for k in range(K):
                    raw_free(k, g)
                    load(k, raw[k][:, :], rows(w_in, k)[:, bass.ds(g * 512 - 3 * 512, 512)])
            for k in range(K):
                raw_free(k, 7)
                load(k, raw[k][:, :], rows(w_in, k)[:, C_R:C_R + 512])
            with sp.Fori(0, HEADS) as i:
                for k in range(K):
                    raw_free(k, i + 8)
                    for b in range(3):
                        load(k, raw[k][:, b * P:(b + 1) * P],
                             rows(w_in, k)[:, bass.ds(i * P + (C_GATE + b * D), P)])
            with sp.Fori(0, 4) as j:
                for u in range(2):
                    for k in range(BR):
                        s = BR * u + k
                        raw_free(s, j + 16)
                        for b, w in enumerate((w_branch_swa, w_branch_moba, w_branch_gla)):
                            load(s, raw[s][:, b * P:(b + 1) * P],
                                 rows(w, k)[:, bass.ds(j * 2 * P + u * P, P)])
            with sp.Fori(0, 2) as c:
                for k in range(K):
                    raw_free(k, c + 20)
                    load(k, raw[k][:, :], rows(w_out, k)[:, bass.ds(c * 512, 512)])
            with sp.Fori(0, FG) as c:
                for k in range(K):
                    raw_free(k, c + 22)
                    load(k, raw[k][:, 0:256], rows(w_ffn_gate, k)[:, bass.ds(c * 256, 256)])
                    load(k, raw[k][:, 256:512], rows(w_ffn_up, k)[:, bass.ds(c * 256, 256)])
            done = K * (22 + FG)
            for k in range(DRING):
                if k < RING:
                    raw_free(k, 22 + FG)
                else:
                    sp.wait_ge(w_steps, ST_D0)
                load(k, raw[k][:, :], rows(w_ffn_down, k)[:, 0:512])
            for n in range(DRING, 2 * FK):
                c, k = divmod(n, FK)
                sp.wait_ge(lo_done, done + n - DRING + 1)
                load(n % DRING, raw[n % DRING][:, :], rows(w_ffn_down, k)[:, c * 512:(c + 1) * 512])
            for n in range(2 * T):
                c, t = divmod(n, T)
                sp.wait_ge(y_out, T + n + 1)
                sp.dma_start(out[0, t * P:(t + 1) * P, c * 512:(c + 1) * 512],
                             X[:, t, c * 512:(c + 1) * 512]).then_inc(out_landed, 16)
            sp.wait_ge(out_landed, 16 * 2 * T)

        @block.gpsimd
        def _(pool):
            nc.gpsimd.memset(ident[:, :], 0.0).then_inc(gate_read, 1)
            nc.gpsimd.memset(wmask[:, :], 0.0).then_inc(y_ready, 1)
            nc.gpsimd.memset(once[:, :], 1.0).then_inc(consts, 1)
            pool.wait_ge(consts, 1)
            nc.gpsimd.affine_select(out=ident[:, :], in_=ident[:, :], compare_op=ALU.not_equal, fill=1.0,
                                    base=0, pattern=[[-1, P]], channel_multiplier=1).then_inc(consts, 1)
            nc.gpsimd.affine_select(out=wmask[:, 0:P], in_=wmask[:, 0:P], compare_op=ALU.is_gt, fill=NEG,
                                    base=0, pattern=[[1, P]], channel_multiplier=-1)
            nc.gpsimd.affine_select(out=wmask[:, P:], in_=wmask[:, P:], compare_op=ALU.is_ge, fill=NEG,
                                    base=0, pattern=[[-1, P]], channel_multiplier=1)
            half = HD // 2
            for n in range(half):
                f = float(np.float32(10000.0) ** np.float32(-2.0 * n / HD))
                ins = nc.gpsimd.memset(invf[:, n:n + 1], f)
                if n < 3:
                    ins.then_inc(*((merge_read, 2), (f_read, 3), (y_out, T))[n])
            nc.gpsimd.memset(once[:, 0:S:GC], 0.0).then_inc(qk_T, 1)
            nc.gpsimd.memset(cm[:, :], 1.0).then_inc(consts, 1)
            pool.wait_ge(consts, 3)
            nc.gpsimd.tensor_copy(identb[:, :], ident[:, :])
            nc.gpsimd.affine_select(out=cm[:, :], in_=cm[:, :], compare_op=ALU.is_ge, fill=0.0,
                                    base=0, pattern=[[1, P]], channel_multiplier=-1).then_inc(consts, 1)
            pool.wait_ge(consts, 4)
            nc.gpsimd.memset(cm[0:GC, GC:P], 0.0).then_inc(consts, 1)
            pool.wait_ge(consts, 5)
            nc.gpsimd.tensor_copy(cmask[:, :], cm[:, :]).then_inc(consts, 1)
            nc.gpsimd.memset(am[:, :, :, :, :], 0.0).then_inc(am_zero, 1)
            nc.gpsimd.memset(st[:, :, 0, :], 0.0).then_inc(am_zero, 1)

            def split(g, s, width):
                pool.wait_ge(hi_done, g + 1)
                nc.gpsimd.tensor_tensor(wlo[s][:, 0:width], raw[s][:, 0:width],
                                        whi[s][:, 0:width].bitcast(F32), ALU.subtract).then_inc(lo_done, 1)

            for k in range(K):
                split(k, k, 512)
            for k in range(K):
                split(K + k, k, 272)
            with pool.Fori(2, 8) as g:
                for k in range(K):
                    split(g * K + k, k, 512)
            with pool.Fori(8, 20) as g:
                for k in range(K):
                    split(g * K + k, k, 384)
            with pool.Fori(20, 22 + FG) as g:
                for k in range(K):
                    split(g * K + k, k, 512)
            with pool.Fori(0, 2 * FK // DRING) as h:
                for s in range(DRING):
                    split(h * DRING + (K * (22 + FG) + s), s, 512)

        @block.scalar
        def _(act):
            seq = [0]

            def link(ins):
                seq[0] += 1
                ins.then_inc(act_seq, 1)
                act.wait_ge(act_seq, seq[0])

            def rnd(s, width, landed):
                act.wait_ge(w_landed[s], landed)
                nc.scalar.activation(whi[s][:, 0:width], raw[s][:, 0:width], ACT.Copy).then_inc(hi_done, 1)

            def rnd_after(group, ks, width, landed=None):
                for k in ks:
                    act.wait_ge(w_steps, ST_G * (group - 1) + (k + 1 if k < K - 1 else ST_G))
                    rnd(k, width, landed or 16 * (group + 1))

            def square_sums(src, t, c, done, width):
                if done:
                    act.wait_ge(x_squared, done)
                nc.scalar.activation(sqx[:, 0:width], src, ACT.Square,
                                     accum_out=ss[:, c * T + t:c * T + t + 1]).then_inc(x_squared, 1)

            def gained_hi(dst, k, done):
                act.wait_ge(x_T, done + k + 1)
                nc.scalar.activation(dst[:, k, :], PS[:, 4 + k % 4, :], ACT.Copy,
                                     scale=vT[:, done + k:done + k + 1]).then_inc(hT_hi, 1)

            def copy_out(group, t):
                act.wait_ge(w_steps, ST_G * group + K + t)
                c = (group - 3) * 512
                nc.scalar.activation(nat[:, t, c:c + 512], PS[:, t, :], ACT.Copy).then_inc(acc_free, 1)

            def rope_squares(n):
                act.wait_ge(acc_free, 4 * (n + 4))
                if n:
                    act.wait_ge(sqr_read, n)
                h0 = 0
                for c0, heads, _ in CHUNKS[n]:
                    last = nc.scalar.activation(sqr[:, :, h0:h0 + heads, :], nat[:, :, c0:c0 + heads * HD]
                                                .rearrange("p t (h d) -> p t h d", d=HD), ACT.Square)
                    h0 += heads
                last.then_inc(rope_sq, 1)

            for t in range(T):
                act.wait_ge(x_landed[t], 16)
                square_sums(X0[:, t, :], t, 0, t, D)
            AHEAD = 3
            for k in range(AHEAD):
                rnd(k, 512, 16)
            act.wait_ge(vec_ready, 2)
            for k in range(K):
                gained_hi(hT_h, k, 0)
                if k + AHEAD < K:
                    rnd(k + AHEAD, 512, 16)
            act.wait_ge(ang_ready, 1)
            for n in range(2):
                nc.scalar.activation(ang[:, n, :, :], ang[:, n, :, :], ACT.Sin).then_inc(sin_done, 1)
            rnd_after(1, range(K), 272)
            rnd_after(2, range(K), 512)
            rnd_after(3, range(5), 512)
            for p in range(2):
                act.wait_ge(z_read, p + 1)
                link(nc.scalar.activation(gx[:, p, :], PS[:, 5 + p, :], ACT.Abs, bias=vT[:, 16 + p:17 + p]))
            for p in range(2):
                link(nc.scalar.activation(gx[:, p, :], gx[:, p, :], ACT.Exp, scale=-1.0))
            for p in range(2):
                nc.scalar.activation(gx[:, p, :], gx[:, p, :], ACT.Ln, bias=1.0).then_inc(soft_done, 1)
            rnd_after(3, range(5, K), 512)
            act.wait_ge(b_ready, 2)
            for p in range(2):
                nc.scalar.activation(gx[:, p, :], lab[:, p, :], ACT.Exp, scale=1 / 16).then_inc(gexp, 1)
                nc.scalar.activation(dec[:, p, :], lab[:, p, GC - 1:S:GC], ACT.Exp,
                                     scale=1 / 16).then_inc(gexp, 1)
            for p in range(2):
                act.wait_ge(b_ready, p + 3)
                act.wait_ge(gexp_used, p + 1)
                nc.scalar.activation(gx[:, p, :], kt[:, p, :], ACT.Exp, scale=1 / 16).then_inc(gexp, 1)
            for p in range(2):
                act.wait_ge(gexp_used, p + 3)
                nc.scalar.activation(gx[:, p, :], lab[:, p, :], ACT.Exp, scale=-1 / 16).then_inc(gexp, 1)
            for g in range(3, 7):
                rnd_after(g + 1, range(5), 512)
                if g == 4:
                    for t in range(T):
                        act.wait_ge(o_done, t + 1)
                        nc.scalar.activation(natv[:, t, 0:BW], PS[:, 4 + t, :], ACT.Copy).then_inc(o_copied, 1)
                        nc.scalar.activation(osq[:, t, :], PS[:, 4 + t, :], ACT.Square).then_inc(o_squared, 1)
                rnd_after(g + 1, range(5, K - 1), 512)
                for t in range(T):
                    copy_out(g, t)
                rnd_after(g + 1, [K - 1], 512)
                rope_squares(g - 3)
            rnd_after(8, range(K - 1), 384, LD_G + 48)
            for j in range(BR):
                act.wait_ge(w_steps, ST_G * 7 + K + j)
                nc.scalar.activation(srT[:, R_ORDER[j], :], PS[:, R_ORDER[j], :], ACT.Tanh,
                                     scale=0.5).then_inc(r_tanh, 1)
            rnd_after(8, [K - 1], 384, LD_G + 48)

            with act.Fori(0, KV) as g:
                act.wait_ge(rope_done, 4)
                act.wait_ge(qk_T, g * (2 * GPK) + 1)
                nc.scalar.activation(stg[:, :, 1, 0, :], nat[:, :, bass.ds(g * HD + C_KA, HD)],
                                     ACT.Copy).then_inc(kstaged, 1)
                with act.Fori(0, GPK) as m:
                    h = g * GPK + m
                    act.wait_ge(qk_T, h * 2 + 1)
                    for n, c0, br in ((0, C_QA, 0), (0, C_QB, 1), (1, C_KB, 1)):
                        nc.scalar.activation(stg[:, :, n, br, :], nat[:, :, bass.ds(h * HD + c0, HD)],
                                             ACT.Copy).then_inc(staged, 1)

                    def gate(b, bank, step):
                        act.wait_ge(w_steps, h * ST_HEAD + (ST_GATE0 + step))
                        nc.scalar.activation(tg[:, bass.ds(h, 1), b, :], PS[:, bank, :], ACT.Tanh,
                                             scale=0.5).then_inc(gate_read, 1)

                    gate(0, 0, 1)
                    act.wait_ge(negmax, h * 2 + 1)
                    for t in (0, 2, 1, 3):
                        bank, col = M_AT[t]
                        n = M_PR[t] * P
                        w = (t + 1) * P
                        nc.scalar.activation(pr[:, n:n + w], PS[:, bank, col:col + w], ACT.Exp,
                                             bias=mx[:, t:t + 1], accum_out=den[:, t:t + 1]).then_inc(probs, 1)
                    act.wait_ge(negmax, h * 2 + 2)
                    for t in (1, 2, 3, 0):
                        bank, col = S_AT[t]
                        n = S_PR[t] * P
                        w = P if t == 0 else 2 * P
                        nc.scalar.activation(pr[:, n:n + w], PS[:, bank, col:col + w], ACT.Exp,
                                             bias=mx[:, 4 + t:5 + t],
                                             accum_out=den[:, 4 + t:5 + t]).then_inc(probs, 1)
                    nc.scalar.activation(esk[:, :], mx[:, 4:8], ACT.Exp,
                                         bias=sinks[:, bass.ds(h, 1)]).then_inc(probs, 1)
                    gate(1, 1, 2)
                    for n in range(2):
                        bank = 4 + 2 * n
                        act.wait_ge(pr_T, h * 5 + (bank - 2))
                        nc.scalar.activation(prT[:, 4 * (bank - 3):4 * (bank - 3) + 4, :],
                                             PS[:, bank, :], ACT.Copy).then_inc(prT_a, 1)
                    for k in range(K):
                        if k == K - 1:
                            gate(2, 0, ST_HEAD)
                        act.wait_ge(w_steps, h * ST_HEAD + (ST_GATE0 + (3 + k if k < K - 1 else ST_HEAD)))
                        rnd(k, 384, h * 48 + (LD_G + 2 * 48))

            act.wait_ge(pv, HEADS)
            for n in range(BR):
                nc.scalar.activation(yc_h[:, n, :], ycT[:, n, :], ACT.Copy).then_inc(y_hi, 1)
            for i, n in enumerate(Y_ORDER):
                act.wait_ge(y_T, i + 1)
                nc.scalar.activation(ya_h[:, n, :], PS[:, Y_BANK[i], :], ACT.Copy).then_inc(y_hi, 1)
            for t in range(T):
                act.dma_start(X[:, t, :], x[0, t * P:(t + 1) * P, :]).then_inc(x_again, 16)

            def branch_group(j, width, landed):
                for u in range(2):
                    for k in range(BR):
                        s = BR * u + k
                        act.wait_ge(w_steps, j * ST_BR + (ST_BR0 + 6 * u + 3 + k))
                        rnd(s, width, landed)
                    act.wait_ge(merged, j * 2 + (u + 1))
                    nc.scalar.activation(mT_h[:, bass.ds(j * 2 + u, 1), :], mtmp[:, 3, :], ACT.Copy,
                                         scale=0.5).then_inc(m_hi, 1)

            with act.Fori(0, 3) as j:
                branch_group(j, 384, j * 48 + (LD_G + 48 * 10))
            branch_group(3, 512, LD_O + 16)

            def rnd_next(step, ks, landed):
                for k in ks:
                    act.wait_ge(w_steps, step + (k + 1 if k < K - 1 else ST_G))
                    rnd(k, 512, landed)

            def x2_squares(c, t):
                act.wait_ge(acc_free, 4 * (8 + c) + t + 1)
                square_sums(X[:, t, c * 512:(c + 1) * 512], t, c, T * (1 + c) + t, 512)

            for k in range(K):
                act.wait_ge(w_steps, ST_O0 + (k + 1 if k < K - 1 else ST_G))
                rnd(k, 512, LD_O + 32)
            for t in range(T):
                x2_squares(0, t)
            for t in range(T - 1):
                x2_squares(1, t)
            for k in range(K):
                if k == K - 1:
                    x2_squares(1, T - 1)
                act.wait_ge(w_steps, ST_O0 + ST_G + T + k)
                rnd(k, 512, LD_F + 32)
            for k in range(K):
                gained_hi(fT_h, k, K)

            def swiglu(c, u, last):
                step = c * ST_G + ST_F0
                for k in range(K):
                    act.wait_ge(w_steps, step + (k + 1 if k < K - 1 else ST_G))
                    rnd(k, 512, (c * 32 + (LD_F + 64)) if not last else LD_D + 16)
                for f in range(2):
                    act.wait_ge(w_steps, step + (K + 2 * f))
                    nc.scalar.activation(fa[:, f, :], PS[:, 4 * u + f, :], ACT.Tanh,
                                         scale=0.5).then_inc(f_tanh, 1)
                for f in range(2):
                    act.wait_ge(f_read, c * 2 + (3 + f + 1))
                    nc.scalar.activation(aT_h[:, bass.ds(c * 2 + f, 1), :], fa[:, 4 + f, :],
                                         ACT.Copy).then_inc(f_hi, 1)

            with act.Fori(0, FG // 2) as j:
                for u in range(2):
                    swiglu(j * 2 + u, u, False)
            swiglu(FG - 1, 0, True)

            for n in range(RING, 2 * FK):
                s = n % DRING
                if n < DRING:
                    act.wait_ge(w_steps, ST_D0)
                else:
                    c, k = divmod(n - DRING, FK)
                    act.wait_ge(w_steps, ST_D0 + ST_D * c + (k + 1 if k < FK - 1 else ST_D))
                rnd(s, 512, (LD_D if s < RING else 0) + 16 * (n // DRING + 1))

        @block.vector
        def _(dve):
            seq = [0, 0]

            def link(ins):
                seq[1] += 1
                ins.then_inc(dve_seq, 1)
                dve.wait_ge(dve_seq, seq[0] + seq[1])

            V = nc.vector

            def mean_square(a, n, scale):
                return V.tensor_scalar(rv[:, a:n], ss[:, a:n], scale, EPS, ALU.mult, ALU.add)

            def rsqrt(a, n):
                v, y, u = rv[:, a:n], ry[:, a:n], ru[:, a:n]
                link(V.tensor_scalar(y.bitcast(I32), v.bitcast(I32), 1, None, ALU.logical_shift_right))
                link(V.tensor_scalar(y.bitcast(I32), y.bitcast(I32), -1.0, float(0x5F3759DF),
                                     ALU.mult, ALU.add))
                for step in range(3):
                    link(V.tensor_tensor(u, y, y, ALU.mult))
                    link(V.scalar_tensor_tensor(u, u, -0.5, v, ALU.mult, ALU.mult))
                    link(V.scalar_tensor_tensor(y, u, 1.5, y, ALU.add, ALU.mult))

            def diagonals(t0):
                for t in (t0, t0 + 1):
                    last = V.tensor_scalar(diag[:, t, :], ident[:, :], ry[:, t:t + 1], None, ALU.mult)
                last.then_inc(diag_ready, 1)

            def gained_lo(dst_h, dst_l, k, done):
                dve.wait_ge(hT_hi, done + k + 1)
                V.scalar_tensor_tensor(dst_l[:, k, :], PS[:, 4 + k % 4, :], vT[:, done + k:done + k + 1],
                                       dst_h[:, k, :].bitcast(F32), ALU.mult, ALU.subtract).then_inc(hT_done, 1)

            def evacuate(group):
                for t in range(T):
                    dve.wait_ge(w_steps, ST_G * group + K + t)
                    if group == 1:
                        V.tensor_copy(natv[:, t, 256:NV], PS[:, t, 0:272]).then_inc(acc_free, 1)
                    else:
                        V.tensor_copy(nat[:, t, NA - 256:NA], PS[:, t, 0:256])
                        V.tensor_copy(natv[:, t, 0:256], PS[:, t, 256:512]).then_inc(acc_free, 1)

            dve.wait_ge(consts, 2)
            for t0 in (0, 2):
                dve.wait_ge(x_squared, t0 + 2)
                link(mean_square(t0, t0 + 2, 1.0 / D))
                rsqrt(t0, t0 + 2)
                diagonals(t0)
                if t0 == 0:
                    dve.wait_ge(vec_landed, 16 * 5)
                    V.tensor_copy(posf[:, :], posi[:, :]).then_inc(vec_ready, 1)
            dve.wait_ge(vec_T, 1)
            V.tensor_copy(vT[:, :], PS[:, 0, 0:19])
            V.tensor_copy(pT[:, :], PS[:, 0, 32:32 + T]).then_inc(vec_ready, 1)
            dve.wait_ge(vec_ready, 2)
            for k in range(K):
                gained_lo(hT_h, hT_l, k, 0)

            dve.wait_ge(consts, 6)
            half = HD // 2
            a0 = ang[:, 2, :, :]
            link(V.tensor_tensor(a0, pT[:, :].unsqueeze(2).to_broadcast([P, T, half]),
                                 invf[:, :].unsqueeze(1).to_broadcast([P, T, half]), ALU.mult))
            magic = 1.5 * 2.0 ** 23
            two_pi = 2.0 * np.pi
            c1 = 6.28125
            c2 = float(np.float32(np.round((two_pi - c1) * 2 ** 22) / 2 ** 22))
            c3 = float(np.float32(two_pi - c1 - c2))
            for n, (turn, shift) in enumerate(((0.25, np.pi / 2), (0.0, 0.0))):
                r, q = ang[:, n, :, :], ang[:, 3 + n, :, :]
                link(V.tensor_scalar(q, a0, 1.0 / two_pi, turn, ALU.mult, ALU.add))
                link(V.tensor_scalar(q, q, magic, None, ALU.add))
                link(V.tensor_scalar(q, q, magic, None, ALU.subtract))
                link(V.scalar_tensor_tensor(r, q, -c1, a0, ALU.mult, ALU.add))
                link(V.scalar_tensor_tensor(r, q, -c2, r, ALU.mult, ALU.add))
                link(V.scalar_tensor_tensor(r, q, -c3, r, ALU.mult, ALU.add))
                link(V.tensor_scalar(r, r, float(shift), 3.1415925, ALU.add, ALU.min))
                last = V.tensor_scalar(r, r, -3.1415925, None, ALU.max)
                last.then_inc(ang_ready, 1) if n else link(last)

            for j in range(4):
                dve.wait_ge(w_steps, K + j)
                V.tensor_scalar(qk[:, j, :], PS[:, j, :], GDK ** -0.5 if j < 2 else 1.0, None,
                                ALU.mult).then_inc(acc_free, 1)

            dve.wait_ge(small_landed, 16 * 6)
            V.tensor_scalar(nsinks[:, :], sinks[:, :], -1.0, None, ALU.mult)
            V.tensor_scalar(gain[:, 0, :], gain[:, 0, :], HD ** -0.5, None, ALU.mult)
            link(V.tensor_scalar(gain[:, 2, :], gain[:, 2, :], HD ** -0.5, None, ALU.mult))
            dve.wait_ge(sin_done, 2)
            for n in range(4):
                g1 = gain[:, n, 0:half].unsqueeze(1).to_broadcast([P, T, half])
                g2 = gain[:, n, half:HD].unsqueeze(1).to_broadcast([P, T, half])
                V.tensor_tensor(ctab[:, n, :, 0:half], ang[:, 0, :, :], g1, ALU.mult)
                V.tensor_tensor(ctab[:, n, :, half:HD], ang[:, 0, :, :], g2, ALU.mult)
                V.tensor_tensor(stab[:, n, :, 0:half], ang[:, 1, :, :], g1, ALU.mult)
                link(V.tensor_tensor(stab[:, n, :, half:HD], ang[:, 1, :, :], g2, ALU.mult))
                link(V.tensor_scalar(stab[:, n, :, half:HD], stab[:, n, :, half:HD], -1.0, None, ALU.mult))
            evacuate(1)
            dve.wait_ge(low_T, 1)
            V.tensor_copy(alT[:, :], PS[0:RANK, 4, :]).then_inc(low_ready, 1)
            for p in range(2):
                dve.wait_ge(z_done, p + 1)
                V.tensor_scalar(lab[:, p, :], PS[:, 5 + p, :], vT[:, 16 + p:17 + p], 0.0,
                                ALU.add, ALU.min).then_inc(z_read, 1)
            for p in range(2):
                dve.wait_ge(soft_done, p + 1)
                if p == 0:
                    dve.wait_ge(z_read, 2)
                link(V.tensor_tensor(lab[:, p, :], lab[:, p, :], gx[:, p, :], ALU.subtract))
                V.tensor_tensor_scan(lab[:, p, :], once[:, :], lab[:, p, :], 0.0,
                                     ALU.mult, ALU.add).then_inc(b_ready, 1)
            for p in range(2):
                if p == 0:
                    dve.wait_ge(b_ready, 2)
                b3 = lab[:, p, :].rearrange("p (c t) -> p c t", t=GC)
                V.tensor_tensor(kt[:, p, :].rearrange("p (c t) -> p c t", t=GC),
                                b3[:, :, GC - 1:GC].to_broadcast([P, NCH, GC]), b3,
                                ALU.subtract).then_inc(b_ready, 1)
            for p in range(2):
                dve.wait_ge(gexp, 2 * p + 1)
                V.tensor_tensor(qk[:, p, :], qk[:, p, :], gx[:, p, :], ALU.mult).then_inc(gexp_used, 1)
            for p in range(2):
                dve.wait_ge(gexp, 5 + p)
                V.tensor_tensor(kt[:, p, :], qk[:, 2 + p, :], gx[:, p, :], ALU.mult).then_inc(gexp_used, 1)
            for p in range(2):
                dve.wait_ge(gexp, 7 + p)
                V.tensor_tensor(qk[:, 2 + p, :], qk[:, 2 + p, :], gx[:, p, :], ALU.mult).then_inc(gexp_used, 1)

            evacuate(2)
            for n in range(2):
                dve.wait_ge(kt_T, n + 1)
                V.tensor_copy(ktn[:, 2 * n:2 * n + 2, :], PS[:, 4 + n, :]
                              .rearrange("p (t n) -> p t n", t=2)).then_inc(kt_ready, 1)

            def masked(tt):
                for hh in range(2):
                    dve.wait_ge(a_done, 2 * tt + hh + 1)
                    for t in range(2):
                        src = PS[:, 6 + hh, t * 256:(t + 1) * 256].rearrange("p (a n) -> p a n", a=2)
                        last = V.copy_predicated(am[:, 2 * tt + t, hh, :, :],
                                                 cmask[:, :].unsqueeze(1).to_broadcast([P, 2, P]), src)
                    last.then_inc(a_ready, 1)

            dve.wait_ge(am_zero, 2)
            masked(0)
            masked(1)

            def states(p):
                for c in range(NCH - 1):
                    dve.wait_ge(ds_done, 2 * p + c % 2 + 1)
                    last = V.scalar_tensor_tensor(st[:, p, c + 1, :], st[:, p, c, :], dec[:, p, c:c + 1],
                                                  PS[:, 4 + c % 2, (c // 2) * P:(c // 2 + 1) * P],
                                                  ALU.mult, ALU.add)
                    last.then_inc(st_ready, 1) if c == NCH - 2 else link(last)

            states(0)
            states(1)

            def rope(n):
                dve.wait_ge(rope_sq, n + 1)
                parts, h0 = [], 0
                for c0, heads, table in CHUNKS[n]:
                    parts.append((h0, c0, heads, table))
                    last = V.reduce_sum(ss[:, T * h0:T * (h0 + heads)].rearrange("p (t h) -> p t h", h=heads),
                                        sqr[:, :, h0:h0 + heads, :], AX_X)
                    h0 += heads
                last.then_inc(sqr_read, 1)
                dve.wait_ge(sqr_read, n + 1)
                link(mean_square(0, T * h0, 1.0 / HD))
                rsqrt(0, T * h0)

                def view(h0, c0, heads, table):
                    xs = nat[:, :, c0:c0 + heads * HD].rearrange("p t (h d) -> p t h d", d=HD)
                    return (xs, [P, T, heads, HD], ropa[:, :, h0:h0 + heads, :], ropb[:, :, h0:h0 + heads, :],
                            ry[:, T * h0:T * (h0 + heads)].rearrange("p (t h) -> p t h", h=heads))

                for part in parts:
                    xs, full, a, b, rs = view(*part)
                    last = V.tensor_tensor(xs, xs, rs.unsqueeze(3).to_broadcast(full), ALU.mult)
                link(last)
                for part in parts:
                    xs, full, a, b, rs = view(*part)
                    V.tensor_tensor(a, xs, ctab[:, part[3], :, :].unsqueeze(2).to_broadcast(full), ALU.mult)
                    last = V.tensor_tensor(b, xs, stab[:, part[3], :, :].unsqueeze(2).to_broadcast(full),
                                           ALU.mult)
                link(last)
                for part in parts:
                    xs, full, a, b, rs = view(*part)
                    V.tensor_tensor(xs[:, :, :, 0:half], a[:, :, :, 0:half], b[:, :, :, half:HD], ALU.add)
                    last = V.tensor_tensor(xs[:, :, :, half:HD], a[:, :, :, half:HD], b[:, :, :, 0:half],
                                           ALU.add)
                last.then_inc(rope_done, 1)

            rope(0)
            for t in range(T):
                dve.wait_ge(o_squared, t + 1)
                last = V.reduce_sum(ss[:, t * GH:(t + 1) * GH],
                                    osq[:, t, :].rearrange("p (h v) -> p h v", v=GDV), AX_X)
            link(last)
            link(mean_square(0, T * GH, 1.0 / GDV))
            rsqrt(0, T * GH)
            dve.wait_ge(o_copied, T)
            o4 = natv[:, :, 0:BW].rearrange("p t (h v) -> p t h v", v=GDV)
            V.tensor_tensor(o4, o4, ry[:, 0:T * GH].rearrange("p (t h) -> p t h", h=GH).unsqueeze(3)
                            .to_broadcast([P, T, GH, GDV]), ALU.mult).then_inc(o_normed, 1)
            link(V.tensor_scalar(vT[:, 18:19], vT[:, 18:19], 0.5, None, ALU.mult))
            rope(1)
            rope(2)
            rope(3)

            def output_gate(i):
                j = R_ORDER[i]
                dve.wait_ge(r_tanh, i + 1)
                V.scalar_tensor_tensor(srT[:, j, :], srT[:, j, :], 1.0, PS[:, j, :],
                                       ALU.add, ALU.mult).then_inc(acc_free, 1)

            def gated(j):
                V.scalar_tensor_tensor(ycT[:, j, :], PS[:, 4 + j, :], vT[:, 18:19], srT[:, j, :],
                                       ALU.mult, ALU.mult).then_inc(yc_done, 1)

            output_gate(0)
            output_gate(1)
            dve.wait_ge(yc_T, BR)
            dve.wait_ge(acc_free, 29)
            gated(0)
            output_gate(2)
            output_gate(3)
            dve.wait_ge(acc_free, 32)
            for j in range(1, BR):
                gated(j)

            before, LINKS = seq[1], 3
            with dve.Fori(0, KV) as g:
                with dve.Fori(0, GPK) as m:
                    h = g * GPK + m
                    seq[0], seq[1] = h * LINKS, before
                    for n in range(2):
                        dve.wait_ge(qk_T, h * 2 + (n + 2))
                        V.tensor_copy(qkT[:, n, :], PS[:, 3 + n, :]).then_inc(qkT_ready, 1)

                    def top(col, bank, c0, w, count=1):
                        src = PS[:, bank, c0:c0 + w * count]
                        if count > 1:
                            src = src.rearrange("p (a n) -> p a n", a=count)
                        return V.reduce_max(mx[:, col:col + count], src, AX_X, negate=True)

                    dve.wait_ge(scores, h * 5 + 1)
                    top(2, 4, 0, 384)
                    top(0, 4, 384, 128)
                    dve.wait_ge(scores, h * 5 + 2)
                    top(1, 5, 0, 256)
                    dve.wait_ge(scores, h * 5 + 3)
                    top(3, 3, 0, 512).then_inc(negmax, 1)
                    dve.wait_ge(scores, h * 5 + 4)
                    top(5, 6, 0, 256, 2)
                    dve.wait_ge(scores, h * 5 + 5)
                    top(7, 7, 0, 256)
                    link(top(4, 7, 256, 128))
                    V.tensor_scalar(mx[:, 4:8], mx[:, 4:8], nsinks[:, bass.ds(h, 1)], None,
                                    ALU.min).then_inc(negmax, 1)
                    dve.wait_ge(probs, h * 9 + 9)
                    link(V.tensor_tensor(den[:, 4:8], den[:, 4:8], esk[:, :], ALU.add))
                    link(V.reciprocal(rec[:, :], den[:, :]))
                    for bank in (3, 5, 7):
                        dve.wait_ge(pr_T, h * 5 + (bank - 2))
                        n = 4 * (bank - 3)
                        w = min(4, NPR - n)
                        V.tensor_copy(prT[:, n:n + w, :], PS[:, bank, 0:w * P]
                                      .rearrange("p (a n) -> p a n", n=P)).then_inc(prT_v, 1)
                    dve.wait_ge(pv, h + 1)
                    for n, c0 in enumerate((C_QB, C_QA)):
                        V.tensor_tensor(nat[:, :, bass.ds(h * HD + c0, HD)],
                                        PS[:, 2, n * 256:(n + 1) * 256].rearrange("p (t d) -> p t d", d=HD),
                                        rec[:, 4 * n:4 * n + 4].unsqueeze(2).to_broadcast([P, T, HD]),
                                        ALU.mult).then_inc(y_ready, 1)
                    assert seq[1] - before == LINKS
            seq[0], seq[1] = 0, before + HEADS * LINKS

            for n in range(BR):
                dve.wait_ge(y_hi, n + 1)
                V.tensor_tensor(yc_l[:, n, :], ycT[:, n, :], yc_h[:, n, :].bitcast(F32),
                                ALU.subtract).then_inc(y_lo, 1)
            for i, n in enumerate(Y_ORDER):
                dve.wait_ge(y_hi, BR + i + 1)
                V.tensor_tensor(ya_l[:, n, :], PS[:, Y_BANK[i], :], ya_h[:, n, :].bitcast(F32),
                                ALU.subtract).then_inc(y_lo, 1)

            before, LINKS = seq[1], 4
            with dve.Fori(0, 4) as j:
                seq[0], seq[1] = j * LINKS, before
                for u in range(2):
                    for i, b in enumerate(B_ORDER):
                        dve.wait_ge(w_steps, j * ST_BR + (ST_BR0 + 6 * u + (i + 1 if i < 2 else 6)))
                        last = V.scalar_tensor_tensor(mtmp[:, i, :], tg[:, bass.ds(j * 2 + u, 1), b, :], 1.0,
                                                      PS[:, 3 * u + b, :], ALU.add, ALU.mult)
                        if i == 1:
                            link(last)
                            link(V.tensor_tensor(mtmp[:, 0, :], mtmp[:, 0, :], mtmp[:, 1, :], ALU.add))
                    last.then_inc(merge_read, 1)
                    dve.wait_ge(merge_read, j * 2 + (u + 3))
                    V.tensor_tensor(mtmp[:, 3, :], mtmp[:, 0, :], mtmp[:, 2, :], ALU.add).then_inc(merged, 1)
                    dve.wait_ge(m_hi, j * 2 + (u + 1))
                    V.scalar_tensor_tensor(mT_l[:, bass.ds(j * 2 + u, 1), :], mtmp[:, 3, :], 0.5,
                                           mT_h[:, bass.ds(j * 2 + u, 1), :].bitcast(F32),
                                           ALU.mult, ALU.subtract).then_inc(m_lo, 1)
                assert seq[1] - before == LINKS
            seq[0], seq[1] = 0, before + 4 * LINKS

            dve.wait_ge(x_again, 16 * T)
            def residual(c, t, step):
                dve.wait_ge(w_steps, ST_O0 + ST_G * c + step)
                V.tensor_tensor(X[:, t, c * 512:(c + 1) * 512], X[:, t, c * 512:(c + 1) * 512],
                                PS[:, t, :], ALU.add).then_inc(acc_free, 1)

            for t in range(T):
                residual(0, t, K + t)
            dve.wait_ge(x_squared, 2 * T)
            link(mean_square(0, T, 1.0 / D))
            for t in range(T):
                residual(1, t, t + 1 if t < T - 1 else ST_G)
                if t % 2:
                    t0 = t - 1
                    dve.wait_ge(x_squared, 2 * T + t + 1)
                    link(V.scalar_tensor_tensor(rv[:, t0:t0 + 2], ss[:, T + t0:T + t0 + 2], 1.0 / D,
                                                rv[:, t0:t0 + 2], ALU.mult, ALU.add))
                    rsqrt(t0, t0 + 2)
                    diagonals(t0)
            for k in range(K):
                gained_lo(fT_h, fT_l, k, K)

            def swiglu(c, u):
                step = c * ST_G + ST_F0
                for f in range(2):
                    dve.wait_ge(f_tanh, c * 2 + (f + 1))
                    V.scalar_tensor_tensor(fa[:, 2 + f, :], fa[:, f, :], 1.0, PS[:, 4 * u + f, :],
                                           ALU.add, ALU.mult).then_inc(f_mid, 1)
                    dve.wait_ge(f_mid, c * 2 + (f + 1))
                    dve.wait_ge(w_steps, step + (K + 2 * f + 1))
                    V.scalar_tensor_tensor(fa[:, 4 + f, :], fa[:, 2 + f, :], 0.5, PS[:, 4 * u + 2 + f, :],
                                           ALU.mult, ALU.mult).then_inc(f_read, 1)
                for f in range(2):
                    dve.wait_ge(f_hi, c * 2 + (f + 1))
                    V.tensor_tensor(aT_l[:, bass.ds(c * 2 + f, 1), :], fa[:, 4 + f, :],
                                    aT_h[:, bass.ds(c * 2 + f, 1), :].bitcast(F32),
                                    ALU.subtract).then_inc(f_lo, 1)

            with dve.Fori(0, FG // 2) as j:
                for u in range(2):
                    swiglu(j * 2 + u, u)
            swiglu(FG - 1, 0)

            with dve.Fori(0, 2) as c:
                for t in range(T):
                    dve.wait_ge(w_steps, c * ST_D + (ST_D0 + FK + t))
                    part = X[:, t, bass.ds(c * 512, 512)]
                    V.tensor_tensor(part, part, PS[:, 4 + t, :], ALU.add).then_inc(y_out, 1)

        @block.tensor
        def _(pe):
            mm = nc.tensor.matmul

            def three(dst, st_h, st_l, mv_h, mv_l, start, stop):
                mm(dst, st_h, mv_h, start=start, stop=False)
                mm(dst, st_h, mv_l, start=False, stop=False)
                return mm(dst, st_l, mv_h, start=False, stop=stop)

            def four_bank_group(g, free, feature_major, a_h, a_l, width=512, inside=None, banks=0,
                                order=range(4), inputs=None):
                for k in range(K):
                    pe.wait_ge(lo_done, g * K + (k + 1))
                    if inputs:
                        inputs(k)
                    for n in order:
                        if k == 0 and free is not None:
                            pe.wait_ge(acc_free, free + (n + 1))
                        if feature_major:
                            w = slice(n * P, (n + 1) * P)
                            last = three(PS[:, banks + n, :], whi[k][:, w], wlo[k][:, w],
                                         a_h[:, k, :], a_l[:, k, :], k == 0, k == K - 1)
                        else:
                            tok = slice(n * P, (n + 1) * P)
                            last = three(PS[:, banks + n, 0:width], a_h[:, k, tok], a_l[:, k, tok],
                                         whi[k][:, 0:width], wlo[k][:, 0:width], k == 0, k == K - 1)
                        if k == K - 1:
                            last.then_inc(w_steps, 1)
                    if k < K - 1:
                        last.then_inc(w_steps, 1)
                    if inside and k in inside:
                        inside[k]()

            def normed_T(src, k, tiles):
                for t in tiles:
                    last = mm(PS[:, 4 + k % 4, t * P:(t + 1) * P], src[:, t, k * P:(k + 1) * P],
                              diag[:, t, :], start=True, stop=True, skip_group_check=True)
                return last

            def normed_and_first_group(src, done, g, h_h, h_l, order):
                for half in range(2):
                    pe.wait_ge(diag_ready, (2 if done else 0) + half + 1)
                    for k in range(4):
                        last = normed_T(src, k, (2 * half, 2 * half + 1))
                        if half:
                            last.then_inc(x_T, 1)

                def ready(k):
                    pe.wait_ge(hT_done, done + k + 1)

                def later(k):
                    return lambda: normed_T(src, k + 4, range(T)).then_inc(x_T, 1)

                four_bank_group(g, None, True, h_h, h_l, order=order, inputs=ready,
                                inside={k: later(k) for k in range(4)})

            pe.wait_ge(consts, 2)
            pe.wait_ge(vec_ready, 1)
            pe.wait_ge(vec_landed, 16 * 5)
            nc.tensor.transpose(PS[:, 0, 0:19], vecs[:, :], ident[0:19, 0:19])
            nc.tensor.transpose(PS[:, 0, 32:32 + T], posf[:, :], ident[0:T, 0:T]).then_inc(vec_T, 1)
            normed_and_first_group(X0, 0, 0, hT_h, hT_l, range(4))

            def low_transposes():
                pe.wait_ge(acc_free, 8)
                for t in range(T):
                    last = nc.tensor.transpose(PS[0:RANK, 4, t * P:(t + 1) * P],
                                               natv[:, t, LOW:NV], ident[:, :])
                last.then_inc(low_T, 1)

            def decay_logits():
                pe.wait_ge(low_ready, 1)
                for p in range(2):
                    mm(PS[:, 5 + p, :], wal[:, p * P:(p + 1) * P], alT[:, :],
                       start=True, stop=True).then_inc(z_done, 1)

            def a_products(tt):
                for hh in range(2):
                    r = slice(hh * GDK, (hh + 1) * GDK)
                    for t in range(2):
                        tok = slice((2 * tt + t) * P, (2 * tt + t + 1) * P)
                        for p in range(2):
                            c = (2 * t + p) * P
                            last = mm(PS[:, 6 + hh, c:c + P], qk[r, 2 + p, tok], qk[r, p, tok],
                                      start=True, stop=True)
                    last.then_inc(a_done, 1)

            def tails_and_a():
                pe.wait_ge(gexp_used, 6)
                pe.wait_ge(z_read, 2)
                for n in range(2):
                    for t in range(2):
                        for p in range(2):
                            last = nc.tensor.transpose(PS[:, 4 + n, (2 * t + p) * P:(2 * t + p + 1) * P],
                                                       kt[:, p, (2 * n + t) * P:(2 * n + t + 1) * P],
                                                       ident[:, :])
                    last.then_inc(kt_T, 1)
                a_products(0)

            def state_updates(p):
                if p:
                    pe.wait_ge(st_ready, p)
                for par in range(2):
                    r = slice(par * GC, (par + 1) * GC)
                    for t in range(T):
                        for hh in range(2):
                            h = 2 * p + hh
                            last = mm(PS[hh * GDK:(hh + 1) * GDK, 4 + par, t * P:(t + 1) * P],
                                      ktn[r, t, h * GDK:(h + 1) * GDK], natv[r, t, h * GDV:(h + 1) * GDV],
                                      start=True, stop=True)
                    last.then_inc(ds_done, 1)

            def a_and_states():
                pe.wait_ge(kt_ready, 2)
                state_updates(0)
                pe.wait_ge(a_ready, 2)
                a_products(1)

            def outputs():
                pe.wait_ge(a_ready, 4)
                pe.wait_ge(st_ready, 2)
                for hh in range(2):
                    r = slice(hh * GDK, (hh + 1) * GDK)
                    for t in range(T):
                        if hh:
                            pe.wait_ge(o_half, t + 1)
                        for p in range(2):
                            h = 2 * p + hh
                            v = slice(h * GDV, (h + 1) * GDV)
                            mm(PS[:, 4 + t, v], am[:, t, hh, p, :], natv[:, t, v], start=True, stop=False,
                               skip_group_check=True)
                            for ch in range(2):
                                tok = slice(t * P + ch * GC, t * P + (ch + 1) * GC)
                                last = mm(PS[ch * GC:(ch + 1) * GC, 4 + t, v], qk[r, p, tok],
                                          st[r, p, 2 * t + ch, :], start=False, stop=True,
                                          skip_group_check=True)
                        last.then_inc(o_done if hh else o_half, 1)

            def token_group(g, **kw):
                four_bank_group(g, 4 * (g - 1), False, hT_h, hT_l, **kw)

            def gla_transposes():
                pe.wait_ge(o_normed, 1)
                for j in range(BR):
                    for t in range(T):
                        last = nc.tensor.transpose(PS[:, 4 + j, t * P:(t + 1) * P],
                                                   natv[:, t, j * P:(j + 1) * P], ident[:, :])
                    last.then_inc(yc_T, 1)

            token_group(1, width=272)
            token_group(2, inside={1: low_transposes, 4: decay_logits})
            token_group(3, inside={3: tails_and_a, 6: a_and_states})
            token_group(4, inside={1: lambda: state_updates(1), 4: outputs})
            token_group(5)
            token_group(6, inside={1: gla_transposes})
            four_bank_group(7, 4 * 6, True, hT_h, hT_l, order=R_ORDER)

            with pe.Fori(0, KV) as g:
                with pe.Fori(0, GPK) as m:
                    h = g * GPK + m

                    def qk_transposes():
                        pe.wait_ge(acc_free, 30)
                        pe.wait_ge(yc_done, 1)
                        for n in range(2):
                            if n:
                                pe.wait_ge(kstaged, g + 1)
                            pe.wait_ge(staged, h * 3 + (2 + n))
                            for t in range(T):
                                last = nc.tensor.transpose(PS[:, 3 + n, t * P:(t + 1) * P],
                                                           stg[:, t, n, :, :], ident[:, :])
                            last.then_inc(qk_T, 1)

                    def gate_tile(b, bank):
                        for k in range(K):
                            if b == 0 and k == K // 2:
                                qk_transposes()
                            if b == 0:
                                pe.wait_ge(lo_done, h * K + (8 * K + k + 1))
                            w = slice(b * P, (b + 1) * P)
                            last = three(PS[:, bank, :], whi[k][:, w], wlo[k][:, w],
                                         hT_h[:, k, :], hT_l[:, k, :], k == 0, k == K - 1)
                            if b == 2 or k == K - 1:
                                last.then_inc(w_steps, 1)

                    pe.wait_ge(acc_free, 29)
                    pe.wait_ge(gate_read, h * 3 + 1)
                    gate_tile(0, 0)

                    pe.wait_ge(yc_done, BR)
                    pe.wait_ge(acc_free, 32)
                    pe.wait_ge(qkT_ready, h * 2 + 2)

                    def moba_scores(t):
                        bank, col = M_AT[t]
                        w = (t + 1) * P
                        mm(PS[:, bank, col:col + w], qkT[HD:, 0, t * P:(t + 1) * P], qkT[HD:, 1, 0:w],
                           start=True, stop=False)
                        return mm(PS[:, bank, col + w - P:col + w], identb[:, :], wmask[:, P:],
                                  start=False, stop=True)

                    def window_scores(t):
                        bank, col = S_AT[t]
                        k0 = max(0, t - 1) * P
                        w = (t + 1) * P - k0
                        mm(PS[:, bank, col:col + w], qkT[0:HD, 0, t * P:(t + 1) * P], qkT[0:HD, 1, k0:k0 + w],
                           start=True, stop=False)
                        return mm(PS[:, bank, col:col + w], identb[:, :], wmask[:, 2 * P - w:],
                                  start=False, stop=True)

                    moba_scores(2)
                    moba_scores(0).then_inc(scores, 1)
                    moba_scores(1).then_inc(scores, 1)
                    moba_scores(3).then_inc(scores, 1)
                    window_scores(1)
                    window_scores(2).then_inc(scores, 1)
                    window_scores(3)
                    window_scores(0).then_inc(scores, 1)

                    gate_tile(1, 1)
                    pe.wait_ge(probs, h * 9 + 8)
                    for n in range(NPR):
                        last = nc.tensor.transpose(PS[:, 3 + n // 4, (n % 4) * P:(n % 4 + 1) * P],
                                                   pr[:, n * P:(n + 1) * P], ident[:, :])
                        if n % 4 == 3 or n == NPR - 1:
                            last.then_inc(pr_T, 1)
                    pe.wait_ge(gate_read, h * 3 + 2)
                    gate_tile(2, 0)
                    pe.wait_ge(prT_v, h * 3 + 3)
                    pe.wait_ge(prT_a, h * 2 + 2)
                    pe.wait_ge(y_ready, h * 2 + 1)
                    for n, (first, v0, lo) in enumerate(
                            ((M_PR, h * HD + C_VB, lambda t: 0), (S_PR, g * HD + C_VA, lambda t: max(0, t - 1)))):
                        for t in range(T):
                            for kk in range(lo(t), t + 1):
                                last = mm(PS[:, 2, n * 256 + t * HD:n * 256 + (t + 1) * HD],
                                          prT[:, first[t] + kk - lo(t), :], nat[:, kk, bass.ds(v0, HD)],
                                          start=kk == lo(t), stop=kk == t)
                    last.then_inc(pv, 1)

            for i, n in enumerate(Y_ORDER):
                if Y_BANK[i] == 0:
                    pe.wait_ge(gate_read, 3 * HEADS + 1)
                if n in (BR - 1, 2 * BR - 1):
                    pe.wait_ge(y_ready, 2 * HEADS + 1)
                if i == 2 * BR - 1:
                    pe.wait_ge(y_lo, BR + 1)
                c0 = n * P if n < BR else C_QB + (n - BR) * P
                for t in range(T):
                    last = nc.tensor.transpose(PS[:, Y_BANK[i], t * P:(t + 1) * P], nat[:, t, c0:c0 + P],
                                               ident[:, :])
                last.then_inc(y_T, 1)

            with pe.Fori(0, 4) as j:
                for u in range(2):
                    pe.wait_ge(merge_read, j * 2 + (u + 1))
                    for i, b in enumerate(B_ORDER):
                        for k in range(BR):
                            s = BR * u + k
                            if i == 0:
                                pe.wait_ge(lo_done, j * K + (16 * K + s + 1))
                            if u == 0 and i < 2:
                                pe.wait_ge(y_lo, k + 1 if i == 0 else BR + (2 * BR if k == BR - 1 else 6))
                            w = slice(b * P, (b + 1) * P)
                            y_h, y_l, n = (ya_h, ya_l, BR * b + k) if b < 2 else (yc_h, yc_l, k)
                            last = three(PS[:, 3 * u + b, :], whi[s][:, w], wlo[s][:, w],
                                         y_h[:, n, :], y_l[:, n, :], k == 0, k == BR - 1)
                            if i == 2 or k == BR - 1:
                                last.then_inc(w_steps, 1)

            pe.wait_ge(merge_read, 2 + K - 1)

            def merged_part(k):
                if k == 0:
                    pe.wait_ge(merge_read, 2 + K)
                pe.wait_ge(m_lo, k + 1)

            four_bank_group(20, 4 * 7, False, mT_h, mT_l, inputs=merged_part)
            for t in range(T):
                pe.wait_ge(acc_free, 4 * 8 + t + 1)
                for k in range(K):
                    if t == 0:
                        pe.wait_ge(lo_done, 21 * K + k + 1)
                    tok = slice(t * P, (t + 1) * P)
                    last = three(PS[:, t, :], mT_h[:, k, tok], mT_l[:, k, tok], whi[k][:, :], wlo[k][:, :],
                                 k == 0, k == K - 1)
                    if t == T - 1 or k == K - 1:
                        last.then_inc(w_steps, 1)

            normed_and_first_group(X, K, 22, fT_h, fT_l, (0, 2, 1, 3))

            def swiglu(c, u):
                pe.wait_ge(f_read, c * 2 + 1)
                four_bank_group(c + 22, None, True, fT_h, fT_l, banks=4 * u, order=(0, 2, 1, 3))

            with pe.Fori(0, FG // 2) as j:
                for u in range(2):
                    swiglu(j * 2 + (u + 1), 1 - u)

            pe.wait_ge(f_read, 3 + 2 * (FG - 1))
            with pe.Fori(0, 2) as c:
                for k in range(FK):
                    s = k % DRING
                    pe.wait_ge(lo_done, c * FK + (K * (22 + FG) + k + 1))
                    if k in (0, FK - 2, FK - 1):
                        pe.wait_ge(f_lo, k + 1 if k else FK - 2)
                    for t in range(T):
                        if k == 0:
                            pe.wait_ge(y_out, c * T + (t + 1))
                        tok = slice(t * P, (t + 1) * P)
                        last = three(PS[:, 4 + t, :], aT_h[:, k, tok], aT_l[:, k, tok], whi[s][:, :], wlo[s][:, :],
                                     k == 0, k == FK - 1)
                        if k == FK - 1:
                            last.then_inc(w_steps, 1)
                    if k < FK - 1:
                        last.then_inc(w_steps, 1)


_OUT_SHAPE = (1, S, D)
_INS = ["x", "positions", "attn_norm", "w_in", "swa_q_norm", "swa_k_norm", "swa_sinks", "moba_q_norm",
        "moba_k_norm", "gla_w_alpha", "gla_b_alpha", "gla_out_norm", "w_branch_swa", "w_branch_moba",
        "w_branch_gla", "w_out", "ffn_norm", "w_ffn_gate", "w_ffn_up", "w_ffn_down"]
_PLAIN = {"w_in", "w_branch_swa", "w_branch_moba", "w_branch_gla", "w_out", "w_ffn_gate", "w_ffn_up",
          "w_ffn_down"}


def kernel(**inputs):
    import concourse.bacc as bacc
    from concourse.bass_utils import run_bass_kernel_spmd

    nc = bacc.Bacc("TRN2", target_bir_lowering=False, num_devices=1)
    arrays, args = {}, []
    for name in _INS:
        a = np.ascontiguousarray(inputs[name])
        if name in _PLAIN:
            a = a[0]
        arrays[f"in_{name}"] = a
        args.append(nc.dram_tensor(f"in_{name}", a.shape, mybir.dt.from_np(a.dtype), kind="ExternalInput").ap())
    args.append(nc.dram_tensor("out", _OUT_SHAPE, F32, kind="ExternalOutput").ap())
    build_layer(nc, *args)
    r = run_bass_kernel_spmd(nc, [arrays], core_ids=[0])
    return r.results[0]["out"]
```

```python
from contextlib import ExitStack

import numpy as np

import concourse.bass as bass
from concourse import mybir

F32 = mybir.dt.float32
F32R = mybir.dt.float32r
BF16 = mybir.dt.bfloat16
I32 = mybir.dt.int32
ALU = mybir.AluOpType
ACT = mybir.ActivationFunctionType
AX_X = mybir.AxisListType.X

P = 128
D = 1024
S = 512
T = S // P
K = D // P
HD = 64
HEADS = 8
KV = 2
GPK = HEADS // KV
WINDOW = 128
BW = 512
BR = BW // P
GH, GDK, GDV, GC = 4, 64, 128, 64
NCH = S // GC
RANK = 16
F = 2816
FK = F // P
EPS = 1e-6
NEG = -1e30

C_QA, C_KA, C_VA, C_QB, C_KB, C_VB = 0, 512, 640, 768, 1280, 1792
C_QG, C_VG, C_VG2, C_R, C_GATE = 2304, 2816, 3072, 3344, 3856
NA = C_QG
LOW = 512
NV = LOW + RANK

ST_G = K - 1 + 4
ST_GATE0 = 8 * ST_G
ST_HEAD = 2 + K - 1 + 1
ST_BR0 = ST_GATE0 + HEADS * ST_HEAD
ST_BR = 12
ST_O0 = ST_BR0 + 4 * ST_BR
ST_F0 = ST_O0 + 2 * ST_G
FG = F // 256
ST_D0 = ST_F0 + FG * ST_G
ST_D = FK - 1 + T
WARM = (12, 8)
RING = K
DRING = 11
LD_G = 16 * 8
LD_O = LD_G + 48 * 12
LD_F = LD_O + 16 * 2
LD_D = LD_F + 32 * FG


def build_layer(nc, x, positions, attn_norm, w_in, swa_q_norm, swa_k_norm, swa_sinks, moba_q_norm,
                moba_k_norm, gla_w_alpha, gla_b_alpha, gla_out_norm, w_branch_swa, w_branch_moba,
                w_branch_gla, w_out, ffn_norm, w_ffn_gate, w_ffn_up, w_ffn_down, out):
    ctx = ExitStack()
    with ctx:
        def sem(name):
            return ctx.enter_context(nc.semaphore(name))

        base = 16512
        R_RING = base
        R_H = R_RING + 3 * RING * 2048
        R_NAT = R_H + 2 * K * 2048
        R_NATV = R_NAT + T * NA * 4
        R_GT = R_NATV + T * NV * 4
        R_WORK = R_GT + HEADS * 3 * 2048
        R_CONST = R_WORK + 16 * 2048

        def at(name, shape, dt, offset):
            return nc.alloc_sbuf_tensor_at(name, shape, dt, offset=offset)

        raw = [at(f"raw{s}", [P, 512], F32, R_RING + s * 2048) for s in range(RING)]
        whi = [at(f"whi{s}", [P, 512], F32R, R_RING + (RING + s) * 2048) for s in range(RING)]
        wlo = [at(f"wlo{s}", [P, 512], F32R, R_RING + (2 * RING + s) * 2048) for s in range(RING)]
        hT_h = at("hT_h", [P, K, S], F32R, R_H)
        hT_l = at("hT_l", [P, K, S], F32R, R_H + K * 2048)
        ya_h = at("ya_h", [P, 2 * BR, S], F32R, R_H)
        ya_l = at("ya_l", [P, 2 * BR, S], F32R, R_H + K * 2048)
        fT_h = at("fT_h", [P, K, S], F32R, R_H)
        fT_l = at("fT_l", [P, K, S], F32R, R_H + K * 2048)
        for s in range(RING, DRING):
            raw.append(at(f"raw{s}", [P, 512], F32, R_H + (s - RING) * 2048))
            whi.append(at(f"whi{s}", [P, 512], F32R, R_H + (3 + s - RING) * 2048))
            wlo.append(at(f"wlo{s}", [P, 512], F32R, R_H + (6 + s - RING) * 2048))
        nat = at("nat", [P, T, NA], F32, R_NAT)
        natv = at("natv", [P, T, NV], F32, R_NATV)
        mT_h = at("mT_h", [P, K, S], F32R, R_NAT)
        mT_l = at("mT_l", [P, K, S], F32R, R_NAT + K * 2048)
        aT_h = at("aT_h", [P, FK, S], F32R, R_NAT)
        aT_l = at("aT_l", [P, FK, S], F32R, R_NAT + FK * 2048)
        ycT = at("ycT", [P, BR, S], F32, R_NATV)
        mtmp = at("mtmp", [P, 4, S], F32, R_NATV)
        tg = at("tg", [P, HEADS, 3, S], F32, R_GT)
        qk = at("qk", [P, 4, S], F32, R_GT)
        lab = at("lab", [P, 2, S], F32, R_GT + 8192)
        gx = at("gx", [P, 2, S], F32, R_GT + 12288)
        kt = at("kt", [P, 2, S], F32, R_GT + 16384)
        ktn = at("ktn", [P, T, 2 * P], F32, R_GT + 20480)
        st = at("st", [P, 2, NCH, GDV], F32, R_GT + 24576)
        am = at("am", [P, T, 2, 2, P], F32, R_GT + 32768)
        srT = at("srT", [P, BR, S], F32, R_GT + 40960)
        alT = at("alT", [RANK, S], F32, R_GT + 40960)
        once = at("once", [P, S], F32, R_GT + 43008)
        osq = at("osq", [P, T, S], F32, R_GT + 12288)
        ang = at("ang", [P, 6, T, HD // 2], F32, R_GT + 16384)
        cmask = at("cmask", [P, P], I32, R_GT + 45056)
        vecs = at("vecs", [19, P], F32, R_GT)
        cm = at("cm", [P, P], F32, R_NATV)
        posi = at("posi", [T, P], I32, R_GT + 512)
        posf = at("posf", [T, P], F32, R_GT + 1024)
        invf = at("invf", [P, HD // 2], F32, R_GT + 19456)
        gain = at("gain", [P, 4, HD], F32, R_GT + 20480)
        wal = at("wal", [RANK, GH * GDK], F32, R_GT + 21504)
        X0 = at("X0", [P, T, D], F32, R_WORK + 16384)
        sqx = at("sqx", [P, D], F32, R_WORK)
        xn = at("xn", [P, 2, D], F32, R_WORK + 8192)
        ctab = at("ctab", [P, 4, T, HD], F32, R_WORK)
        stab = at("stab", [P, 4, T, HD], F32, R_WORK + 4096)
        ropa = at("ropa", [P, T, HEADS, HD], F32, R_WORK + 8192)
        ropb = at("ropb", [P, T, HEADS, HD], F32, R_WORK + 16384)
        sqr = at("sqr", [P, T, HEADS, HD], F32, R_WORK + 24576)
        NP_M, NP_S = T * (T + 1) // 2, 2 * T - 1
        pr = at("pr", [P, (NP_M + NP_S) * P], F32, R_WORK)
        prT = at("prT", [P, NP_M + NP_S, P], F32, R_WORK + 8704)
        stg = at("stg", [P, T, 2, 2, HD], F32, R_WORK + 17408)
        qkT_h = at("qkT_h", [P, 2, S], F32R, R_WORK + 21504)
        qkT_l = at("qkT_l", [P, 2, S], F32R, R_WORK + 25600)
        yc_h = at("yc_h", [P, BR, S], F32R, R_WORK)
        yc_l = at("yc_l", [P, BR, S], F32R, R_WORK + 8192)
        X = at("X", [P, T, D], F32, R_WORK + 16384)
        fa = at("fa", [P, 8, S], F32, R_WORK)
        off = [R_CONST]

        def small(name, shape, dt):
            n = 1
            for v in shape[1:]:
                n *= v
            t = at(name, shape, dt, off[0])
            off[0] += -(-n * (2 if dt == BF16 else 4) // 32) * 32
            return t

        ident = small("ident", [P, P], F32)
        identb = small("identb", [P, P], BF16)
        wmask = small("wmask", [P, 2 * P], BF16)
        vT = small("vT", [P, 19], F32)
        pT = small("pT", [P, T], F32)
        sinks = small("sinks", [P, HEADS], F32)
        nsinks = small("nsinks", [P, HEADS], F32)
        ss = small("ss", [P, 32], F32)
        rv = small("rv", [P, 32], F32)
        ry = small("ry", [P, 32], F32)
        ru = small("ru", [P, 32], F32)
        mx = small("mx", [P, 8], F32)
        den = small("den", [P, 8], F32)
        esk = small("esk", [P, 4], F32)
        rec = small("rec", [P, 8], F32)
        dec = small("dec", [P, 2, NCH], F32)
        assert off[0] <= 229344, off[0]

        PS = ctx.enter_context(nc.psum_tensor("PS", [P, 8, 512], F32))

        x_landed = [sem(f"x_landed{t}") for t in range(T)]
        vec_landed = sem("vec_landed")
        small_landed = sem("small_landed")
        x_again = sem("x_again")
        w_landed = [sem(f"w_landed{s}") for s in range(DRING)]
        out_landed = sem("out_landed")
        consts = sem("consts")
        am_zero = sem("am_zero")
        lo_done = sem("lo_done")
        hi_done = sem("hi_done")
        w_steps = sem("w_steps")
        act_seq = sem("act_seq")
        dve_seq = sem("dve_seq")
        acc_free = sem("acc_free")
        vec_T = sem("vec_T")
        vec_ready = sem("vec_ready")
        x_squared = sem("x_squared")
        xn_ready = sem("xn_ready")
        x_T = sem("x_T")
        hT_hi = sem("hT_hi")
        hT_done = sem("hT_done")
        ang_ready = sem("ang_ready")
        sin_done = sem("sin_done")
        low_T = sem("low_T")
        low_ready = sem("low_ready")
        z_done = sem("z_done")
        z_read = sem("z_read")
        soft_done = sem("soft_done")
        b_ready = sem("b_ready")
        gexp = sem("gexp")
        gexp_used = sem("gexp_used")
        kt_T = sem("kt_T")
        kt_ready = sem("kt_ready")
        a_done = sem("a_done")
        a_ready = sem("a_ready")
        ds_done = sem("ds_done")
        st_ready = sem("st_ready")
        o_half = sem("o_half")
        o_done = sem("o_done")
        o_copied = sem("o_copied")
        o_squared = sem("o_squared")
        o_normed = sem("o_normed")
        yc_T = sem("yc_T")
        yc_done = sem("yc_done")
        r_tanh = sem("r_tanh")
        rope_sq = sem("rope_sq")
        sqr_read = sem("sqr_read")
        rope_done = sem("rope_done")
        staged = sem("staged")
        kstaged = sem("kstaged")
        qk_T = sem("qk_T")
        qkT_hi = sem("qkT_hi")
        qkT_ready = sem("qkT_ready")
        scores = sem("scores")
        negmax = sem("negmax")
        probs = sem("probs")
        pr_T = sem("pr_T")
        prT_v = sem("prT_v")
        prT_a = sem("prT_a")
        pv = sem("pv")
        y_ready = sem("y_ready")
        gate_read = sem("gate_read")
        y_T = sem("y_T")
        y_hi = sem("y_hi")
        y_lo = sem("y_lo")
        yc_lo = sem("yc_lo")
        merge_read = sem("merge_read")
        merged = sem("merged")
        m_hi = sem("m_hi")
        m_lo = sem("m_lo")
        f_tanh = sem("f_tanh")
        f_mid = sem("f_mid")
        f_read = sem("f_read")
        f_hi = sem("f_hi")
        f_lo = sem("f_lo")
        y_out = sem("y_out")

        block = ctx.enter_context(nc.Block())

        def rows(w, k):
            return w[k * P:(k + 1) * P]

        QUAD = 4 * HD
        CHUNKS = [[(C_QA, HEADS, 0)], [(C_KA, KV, 1), (C_QB, 4, 2)],
                  [(C_QB + QUAD, 4, 2), (C_KB, 4, 3)], [(C_KB + QUAD, 4, 3)]]

        Y_ORDER = (4, 5, 6, 1, 0, 2, 3, 7)
        Y_BANK = (3, 4, 5, 6, 1, 7, 0, 3)
        B_ORDER = (2, 1, 0)
        R_ORDER = (0, 3, 1, 2)

        M_AT = {3: (3, 0), 2: (4, 0), 1: (5, 0), 0: (5, 256)}
        S_AT = {1: (6, 0), 2: (6, 256), 3: (7, 0), 0: (7, 256)}
        M_PR = [t * (t + 1) // 2 for t in range(T)]
        S_PR = [NP_M + max(0, 2 * t - 1) for t in range(T)]
        NPR = NP_M + NP_S

        @block.sync
        def _(sp):
            def load(s, dst, src):
                sp.dma_start(dst, src).then_inc(w_landed[s], 16)

            def raw_free(k, group):
                sp.wait_ge(lo_done, K * (group - 1) + k + 1)

            def load_x(t):
                sp.dma_start(X0[:, t, :], x[0, t * P:(t + 1) * P, :]).then_inc(x_landed[t], 16)

            load_x(0)
            load_x(1)
            for dst, src in ((vecs[0:K, :], attn_norm.rearrange("a (k p) -> (a k) p", p=P)),
                             (vecs[K:2 * K, :], ffn_norm.rearrange("a (k p) -> (a k) p", p=P)),
                             (vecs[16:18, :], gla_b_alpha.rearrange("a (k p) -> (a k) p", p=P)),
                             (vecs[18:19, :], gla_out_norm),
                             (posi[:, :], positions.rearrange("a (k p) -> (a k) p", p=P))):
                sp.dma_start(dst, src).then_inc(vec_landed, 16)
            for k in range(K):
                if k in (2, 4):
                    load_x(k // 2 + 1)
                load(k, raw[k][:, :], rows(w_in, k)[:, C_QG:C_QG + 512])
            for dst, src in ((gain[:, 0, :], swa_q_norm.to_broadcast([P, HD])),
                             (gain[:, 1, :], swa_k_norm.to_broadcast([P, HD])),
                             (gain[:, 2, :], moba_q_norm.to_broadcast([P, HD])),
                             (gain[:, 3, :], moba_k_norm.to_broadcast([P, HD])),
                             (sinks[:, :], swa_sinks.to_broadcast([P, HEADS])),
                             (wal[:, :], gla_w_alpha[0])):
                sp.dma_start(dst, src).then_inc(small_landed, 16)
            for k in range(K):
                raw_free(k, 1)
                load(k, raw[k][:, 0:272], rows(w_in, k)[:, C_VG2:C_VG2 + 272])
            for k in range(K):
                raw_free(k, 2)
                two = rows(w_in, k)[:, C_QG - 256:C_VG + 256]
                src = bass.AP(two.tensor, two.offset, [list(two.ap[0]), [C_VG - C_QG + 256, 2], [1, 256]])
                load(k, raw[k][:, :].rearrange("p (a n) -> p a n", a=2), src)
            with sp.Fori(3, 7) as g:
                for k in range(K):
                    raw_free(k, g)
                    load(k, raw[k][:, :], rows(w_in, k)[:, bass.ds(g * 512 - 3 * 512, 512)])
            for k in range(K):
                raw_free(k, 7)
                load(k, raw[k][:, :], rows(w_in, k)[:, C_R:C_R + 512])
            with sp.Fori(0, HEADS) as i:
                for k in range(K):
                    raw_free(k, i + 8)
                    for b in range(3):
                        load(k, raw[k][:, b * P:(b + 1) * P],
                             rows(w_in, k)[:, bass.ds(i * P + (C_GATE + b * D), P)])
            with sp.Fori(0, 4) as j:
                for u in range(2):
                    for k in range(BR):
                        s = BR * u + k
                        raw_free(s, j + 16)
                        for b, w in enumerate((w_branch_swa, w_branch_moba, w_branch_gla)):
                            load(s, raw[s][:, b * P:(b + 1) * P],
                                 rows(w, k)[:, bass.ds(j * 2 * P + u * P, P)])
            with sp.Fori(0, 2) as c:
                for k in range(K):
                    raw_free(k, c + 20)
                    load(k, raw[k][:, :], rows(w_out, k)[:, bass.ds(c * 512, 512)])
            with sp.Fori(0, FG) as c:
                for k in range(K):
                    raw_free(k, c + 22)
                    load(k, raw[k][:, 0:256], rows(w_ffn_gate, k)[:, bass.ds(c * 256, 256)])
                    load(k, raw[k][:, 256:512], rows(w_ffn_up, k)[:, bass.ds(c * 256, 256)])
            done = K * (22 + FG)
            for k in range(DRING):
                if k < RING:
                    raw_free(k, 22 + FG)
                else:
                    sp.wait_ge(w_steps, ST_D0)
                load(k, raw[k][:, :], rows(w_ffn_down, k)[:, 0:512])
            for n in range(DRING, 2 * FK):
                c, k = divmod(n, FK)
                sp.wait_ge(lo_done, done + n - DRING + 1)
                load(n % DRING, raw[n % DRING][:, :], rows(w_ffn_down, k)[:, c * 512:(c + 1) * 512])
            for n in range(2 * T):
                c, t = divmod(n, T)
                sp.wait_ge(y_out, T + n + 1)
                sp.dma_start(out[0, t * P:(t + 1) * P, c * 512:(c + 1) * 512],
                             X[:, t, c * 512:(c + 1) * 512]).then_inc(out_landed, 16)
            sp.wait_ge(out_landed, 16 * 2 * T)

        @block.gpsimd
        def _(pool):
            nc.gpsimd.memset(ident[:, :], 0.0).then_inc(gate_read, 1)
            nc.gpsimd.memset(wmask[:, :], 0.0).then_inc(y_ready, 1)
            nc.gpsimd.memset(once[:, :], 1.0).then_inc(consts, 1)
            pool.wait_ge(consts, 1)
            nc.gpsimd.affine_select(out=ident[:, :], in_=ident[:, :], compare_op=ALU.not_equal, fill=1.0,
                                    base=0, pattern=[[-1, P]], channel_multiplier=1).then_inc(consts, 1)
            nc.gpsimd.affine_select(out=wmask[:, 0:P], in_=wmask[:, 0:P], compare_op=ALU.is_gt, fill=NEG,
                                    base=0, pattern=[[1, P]], channel_multiplier=-1)
            nc.gpsimd.affine_select(out=wmask[:, P:], in_=wmask[:, P:], compare_op=ALU.is_ge, fill=NEG,
                                    base=0, pattern=[[-1, P]], channel_multiplier=1)
            half = HD // 2
            for n in range(half):
                f = float(np.float32(10000.0) ** np.float32(-2.0 * n / HD))
                ins = nc.gpsimd.memset(invf[:, n:n + 1], f)
                if n < 3:
                    ins.then_inc(*((merge_read, 2), (f_read, 3), (y_out, T))[n])
            nc.gpsimd.memset(once[:, 0:S:GC], 0.0).then_inc(qk_T, 1)
            nc.gpsimd.memset(cm[:, :], 1.0).then_inc(consts, 1)
            pool.wait_ge(consts, 3)
            nc.gpsimd.tensor_copy(identb[:, :], ident[:, :])
            nc.gpsimd.affine_select(out=cm[:, :], in_=cm[:, :], compare_op=ALU.is_ge, fill=0.0,
                                    base=0, pattern=[[1, P]], channel_multiplier=-1).then_inc(consts, 1)
            pool.wait_ge(consts, 4)
            nc.gpsimd.memset(cm[0:GC, GC:P], 0.0).then_inc(consts, 1)
            pool.wait_ge(consts, 5)
            nc.gpsimd.tensor_copy(cmask[:, :], cm[:, :]).then_inc(consts, 1)
            nc.gpsimd.memset(am[:, :, :, :, :], 0.0).then_inc(am_zero, 1)
            nc.gpsimd.memset(st[:, :, 0, :], 0.0).then_inc(am_zero, 1)

            def split(g, s, width):
                pool.wait_ge(hi_done, g + 1)
                nc.gpsimd.tensor_tensor(wlo[s][:, 0:width], raw[s][:, 0:width],
                                        whi[s][:, 0:width].bitcast(F32), ALU.subtract).then_inc(lo_done, 1)

            for k in range(K):
                split(k, k, 512)
            for k in range(K):
                split(K + k, k, 272)
            with pool.Fori(2, 8) as g:
                for k in range(K):
                    split(g * K + k, k, 512)
            with pool.Fori(8, 17) as g:
                for k in range(K):
                    split(g * K + k, k, 384)
            for b in (2, 3):
                pool.wait_ge(y_hi, b + 2)
                nc.gpsimd.tensor_tensor(yc_l[:, b, :], ycT[:, b, :], yc_h[:, b, :].bitcast(F32),
                                        ALU.subtract).then_inc(yc_lo, 1)
            with pool.Fori(17, 20) as g:
                for k in range(K):
                    split(g * K + k, k, 384)
            with pool.Fori(20, 22 + FG) as g:
                for k in range(K):
                    split(g * K + k, k, 512)
            with pool.Fori(0, 2 * FK // DRING) as h:
                for s in range(DRING):
                    split(h * DRING + (K * (22 + FG) + s), s, 512)

        @block.scalar
        def _(act):
            seq = [0]

            def link(ins):
                seq[0] += 1
                ins.then_inc(act_seq, 1)
                act.wait_ge(act_seq, seq[0])

            def rnd(s, width, landed):
                act.wait_ge(w_landed[s], landed)
                nc.scalar.activation(whi[s][:, 0:width], raw[s][:, 0:width], ACT.Copy).then_inc(hi_done, 1)

            def rnd_after(group, ks, width, landed=None):
                for k in ks:
                    act.wait_ge(w_steps, ST_G * (group - 1) + (k + 1 if k < K - 1 else ST_G))
                    rnd(k, width, landed or 16 * (group + 1))

            def square_sums(src, t, c, done, width):
                if done:
                    act.wait_ge(x_squared, done)
                nc.scalar.activation(sqx[:, 0:width], src, ACT.Square,
                                     accum_out=ss[:, c * T + t:c * T + t + 1]).then_inc(x_squared, 1)

            def gained_hi(dst, norm, half, k):
                act.wait_ge(x_T, 8 * norm + 4 * half + k // 2 + 1)
                nc.scalar.activation(dst[:, k, half * 256:(half + 1) * 256],
                                     PS[:, 4 + k // 2, (k % 2) * 256:(k % 2 + 1) * 256], ACT.Copy,
                                     scale=vT[:, K * norm + k:K * norm + k + 1]).then_inc(hT_hi, 1)

            def copy_out(group, t):
                act.wait_ge(w_steps, ST_G * group + K + t)
                c = (group - 3) * 512
                nc.scalar.activation(nat[:, t, c:c + 512], PS[:, t, :], ACT.Copy).then_inc(acc_free, 1)

            def rope_squares(n):
                act.wait_ge(acc_free, 4 * (n + 4))
                if n:
                    act.wait_ge(sqr_read, n)
                h0 = 0
                for c0, heads, _ in CHUNKS[n]:
                    last = nc.scalar.activation(sqr[:, :, h0:h0 + heads, :], nat[:, :, c0:c0 + heads * HD]
                                                .rearrange("p t (h d) -> p t h d", d=HD), ACT.Square)
                    h0 += heads
                last.then_inc(rope_sq, 1)

            def x_squares(t):
                act.wait_ge(x_landed[t], 16)
                square_sums(X0[:, t, :], t, 0, t, D)

            x_squares(0)
            x_squares(1)
            rnd(0, 512, 16)
            rnd(1, 512, 16)
            x_squares(2)
            act.wait_ge(vec_ready, 2)
            for k in range(K):
                gained_hi(hT_h, 0, 0, k)
                if k == 3:
                    x_squares(3)
                if k < K - 1 and k:
                    rnd(k + 1, 512, 16)
            for k in range(K):
                gained_hi(hT_h, 0, 1, k)
            act.wait_ge(ang_ready, 1)
            for n in range(2):
                nc.scalar.activation(ang[:, n, :, :], ang[:, n, :, :], ACT.Sin).then_inc(sin_done, 1)
            rnd_after(1, range(K), 272)
            rnd_after(2, range(K), 512)
            rnd_after(3, range(3), 512)
            for p in range(2):
                act.wait_ge(z_read, p + 1)
                link(nc.scalar.activation(gx[:, p, :], PS[:, 5 + p, :], ACT.Abs, bias=vT[:, 16 + p:17 + p]))
            for p in range(2):
                link(nc.scalar.activation(gx[:, p, :], gx[:, p, :], ACT.Exp, scale=-1.0))
            for p in range(2):
                nc.scalar.activation(gx[:, p, :], gx[:, p, :], ACT.Ln, bias=1.0).then_inc(soft_done, 1)
            rnd_after(3, range(3, 6), 512)
            act.wait_ge(b_ready, 2)
            for p in range(2):
                nc.scalar.activation(gx[:, p, :], lab[:, p, :], ACT.Exp, scale=1 / 16).then_inc(gexp, 1)
                nc.scalar.activation(dec[:, p, :], lab[:, p, GC - 1:S:GC], ACT.Exp,
                                     scale=1 / 16).then_inc(gexp, 1)
            for p in range(2):
                act.wait_ge(b_ready, p + 3)
                act.wait_ge(gexp_used, p + 1)
                nc.scalar.activation(gx[:, p, :], kt[:, p, :], ACT.Exp, scale=1 / 16).then_inc(gexp, 1)
            for p in range(2):
                act.wait_ge(gexp_used, p + 3)
                nc.scalar.activation(gx[:, p, :], lab[:, p, :], ACT.Exp, scale=-1 / 16).then_inc(gexp, 1)
            rnd_after(3, range(6, K), 512)
            for g in range(3, 7):
                rnd_after(g + 1, range(5), 512)
                if g == 4:
                    for t in range(T):
                        act.wait_ge(o_done, t + 1)
                        nc.scalar.activation(natv[:, t, 0:BW], PS[:, 4 + t, :], ACT.Copy).then_inc(o_copied, 1)
                        nc.scalar.activation(osq[:, t, :], PS[:, 4 + t, :], ACT.Square).then_inc(o_squared, 1)
                rnd_after(g + 1, range(5, K - 1), 512)
                for t in range(T):
                    copy_out(g, t)
                rnd_after(g + 1, [K - 1], 512)
                rope_squares(g - 3)
            rnd_after(8, range(K - 1), 384, LD_G + 48)
            for j in range(BR):
                act.wait_ge(w_steps, ST_G * 7 + K + j)
                nc.scalar.activation(srT[:, R_ORDER[j], :], PS[:, R_ORDER[j], :], ACT.Tanh,
                                     scale=0.5).then_inc(r_tanh, 1)
            rnd_after(8, [K - 1], 384, LD_G + 48)

            with act.Fori(0, KV) as g:
                act.wait_ge(rope_done, 4)
                act.wait_ge(qk_T, g * (2 * GPK) + 1)
                nc.scalar.activation(stg[:, :, 1, 0, :], nat[:, :, bass.ds(g * HD + C_KA, HD)],
                                     ACT.Copy).then_inc(kstaged, 1)
                with act.Fori(0, GPK) as m:
                    h = g * GPK + m
                    act.wait_ge(qk_T, h * 2 + 1)
                    for n, c0, br in ((0, C_QA, 0), (0, C_QB, 1), (1, C_KB, 1)):
                        nc.scalar.activation(stg[:, :, n, br, :], nat[:, :, bass.ds(h * HD + c0, HD)],
                                             ACT.Copy).then_inc(staged, 1)
                    for n in range(2):
                        act.wait_ge(qk_T, h * 2 + (n + 2))
                        nc.scalar.activation(qkT_h[:, n, :], PS[:, 3 + n, :], ACT.Copy).then_inc(qkT_hi, 1)

                    def gate(b, bank, step):
                        act.wait_ge(w_steps, h * ST_HEAD + (ST_GATE0 + step))
                        nc.scalar.activation(tg[:, bass.ds(h, 1), b, :], PS[:, bank, :], ACT.Tanh,
                                             scale=0.5).then_inc(gate_read, 1)

                    gate(0, 0, 1)
                    act.wait_ge(negmax, h * 2 + 1)
                    for t in (0, 2, 1, 3):
                        bank, col = M_AT[t]
                        n = M_PR[t] * P
                        w = (t + 1) * P
                        nc.scalar.activation(pr[:, n:n + w], PS[:, bank, col:col + w], ACT.Exp,
                                             bias=mx[:, t:t + 1], accum_out=den[:, t:t + 1]).then_inc(probs, 1)
                    act.wait_ge(negmax, h * 2 + 2)
                    for t in (1, 2, 3, 0):
                        bank, col = S_AT[t]
                        n = S_PR[t] * P
                        w = P if t == 0 else 2 * P
                        nc.scalar.activation(pr[:, n:n + w], PS[:, bank, col:col + w], ACT.Exp,
                                             bias=mx[:, 4 + t:5 + t],
                                             accum_out=den[:, 4 + t:5 + t]).then_inc(probs, 1)
                    nc.scalar.activation(esk[:, :], mx[:, 4:8], ACT.Exp,
                                         bias=sinks[:, bass.ds(h, 1)]).then_inc(probs, 1)
                    gate(1, 1, 2)
                    for n in range(2):
                        bank = 4 + 2 * n
                        act.wait_ge(pr_T, h * 5 + (bank - 2))
                        nc.scalar.activation(prT[:, 4 * (bank - 3):4 * (bank - 3) + 4, :],
                                             PS[:, bank, :], ACT.Copy).then_inc(prT_a, 1)
                    for k in range(K):
                        if k == K - 1:
                            gate(2, 0, ST_HEAD)
                        act.wait_ge(w_steps, h * ST_HEAD + (ST_GATE0 + (3 + k if k < K - 1 else ST_HEAD)))
                        rnd(k, 384, h * 48 + (LD_G + 2 * 48))

            for i, n in enumerate(Y_ORDER):
                act.wait_ge(y_T, i + 1)
                nc.scalar.activation(ya_h[:, n, :], PS[:, Y_BANK[i], :], ACT.Copy).then_inc(y_hi, 1)
                if i == 0:
                    for b in range(BR):
                        nc.scalar.activation(yc_h[:, b, :], ycT[:, b, :], ACT.Copy).then_inc(y_hi, 1)
            for t in range(T):
                act.dma_start(X[:, t, :], x[0, t * P:(t + 1) * P, :]).then_inc(x_again, 16)

            def branch_group(j, width, landed):
                for u in range(2):
                    for k in range(BR):
                        s = BR * u + k
                        act.wait_ge(w_steps, j * ST_BR + (ST_BR0 + 6 * u + 3 + k))
                        rnd(s, width, landed)
                    act.wait_ge(merged, j * 2 + (u + 1))
                    nc.scalar.activation(mT_h[:, bass.ds(j * 2 + u, 1), :], mtmp[:, 3, :], ACT.Copy,
                                         scale=0.5).then_inc(m_hi, 1)

            with act.Fori(0, 3) as j:
                branch_group(j, 384, j * 48 + (LD_G + 48 * 10))
            branch_group(3, 512, LD_O + 16)

            def rnd_next(step, ks, landed):
                for k in ks:
                    act.wait_ge(w_steps, step + (k + 1 if k < K - 1 else ST_G))
                    rnd(k, 512, landed)

            def x2_squares(c, t):
                act.wait_ge(acc_free, 4 * (8 + c) + t + 1)
                square_sums(X[:, t, c * 512:(c + 1) * 512], t, c, T * (1 + c) + t, 512)

            for k in range(K):
                act.wait_ge(w_steps, ST_O0 + (k + 1 if k < K - 1 else ST_G))
                rnd(k, 512, LD_O + 32)
            for t in range(T):
                x2_squares(0, t)
            for t in range(T - 1):
                x2_squares(1, t)
            for k in range(K):
                gained_hi(fT_h, 1, 0, k)
            for k in range(K):
                if k == K - 2:
                    x2_squares(1, T - 1)
                act.wait_ge(w_steps, ST_O0 + ST_G + T + k)
                rnd(k, 512, LD_F + 32)
            for k in range(K):
                gained_hi(fT_h, 1, 1, k)

            def swiglu(c, u, last):
                step = c * ST_G + ST_F0
                for k in range(K):
                    act.wait_ge(w_steps, step + (k + 1 if k < K - 1 else ST_G))
                    rnd(k, 512, (c * 32 + (LD_F + 64)) if not last else LD_D + 16)
                for f in range(2):
                    act.wait_ge(w_steps, step + (K + 2 * f))
                    nc.scalar.activation(fa[:, f, :], PS[:, 4 * u + f, :], ACT.Tanh,
                                         scale=0.5).then_inc(f_tanh, 1)
                for f in range(2):
                    act.wait_ge(f_read, c * 2 + (3 + f + 1))
                    nc.scalar.activation(aT_h[:, bass.ds(c * 2 + f, 1), :], fa[:, 4 + f, :],
                                         ACT.Copy).then_inc(f_hi, 1)

            with act.Fori(0, FG // 2) as j:
                for u in range(2):
                    swiglu(j * 2 + u, u, False)
            swiglu(FG - 1, 0, True)

            for n in range(RING, 2 * FK):
                s = n % DRING
                if n < DRING:
                    act.wait_ge(w_steps, ST_D0)
                else:
                    c, k = divmod(n - DRING, FK)
                    act.wait_ge(w_steps, ST_D0 + ST_D * c + (k + 1 if k < FK - 1 else ST_D))
                rnd(s, 512, (LD_D if s < RING else 0) + 16 * (n // DRING + 1))

        @block.vector
        def _(dve):
            seq = [0, 0]

            def link(ins):
                seq[1] += 1
                ins.then_inc(dve_seq, 1)
                dve.wait_ge(dve_seq, seq[0] + seq[1])

            V = nc.vector
            FACTOR = 64 / 9

            def mean_square(a, n, scale):
                return V.tensor_scalar(rv[:, a:n], ss[:, a:n], FACTOR * scale, FACTOR * EPS, ALU.mult, ALU.add)

            def rsqrt(a, n):
                v, y, u = rv[:, a:n], ry[:, a:n], ru[:, a:n]
                link(V.tensor_scalar(y.bitcast(I32), v.bitcast(I32), 1, None, ALU.logical_shift_right))
                link(V.tensor_scalar(y.bitcast(I32), y.bitcast(I32), -1.0, float(0x5F3759DF),
                                     ALU.mult, ALU.add))
                link(V.tensor_tensor(u, y, y, ALU.mult))
                link(V.scalar_tensor_tensor(u, u, -0.5, v, ALU.mult, ALU.mult))
                link(V.scalar_tensor_tensor(y, u, 1.5, y, ALU.add, ALU.mult))
                link(V.tensor_tensor(u, y, y, ALU.mult))
                link(V.tensor_tensor(u, u, v, ALU.mult))
                link(V.scalar_tensor_tensor(u, u, -10 / 3, u, ALU.add, ALU.mult))
                link(V.scalar_tensor_tensor(y, u, 5.0, y, ALU.add, ALU.mult))

            def normed(src, norm, half, columns=range(2)):
                if half:
                    dve.wait_ge(x_T, 8 * norm + 4)
                for c in columns:
                    for tt in range(2):
                        t = 2 * half + tt
                        last = V.tensor_scalar(xn[:, tt, c * 512:(c + 1) * 512],
                                               src[:, t, c * 512:(c + 1) * 512], ry[:, t:t + 1], None, ALU.mult)
                    last.then_inc(xn_ready, 1)

            def gained_lo(dst_h, dst_l, norm, half, k):
                if k % 2 == 0:
                    dve.wait_ge(hT_hi, 16 * norm + 8 * half + k + 2)
                tok = slice(half * 256, (half + 1) * 256)
                V.scalar_tensor_tensor(dst_l[:, k, tok], PS[:, 4 + k // 2, (k % 2) * 256:(k % 2 + 1) * 256],
                                       vT[:, K * norm + k:K * norm + k + 1], dst_h[:, k, tok].bitcast(F32),
                                       ALU.mult, ALU.subtract).then_inc(hT_done, 1)

            def evacuate(group):
                for t in range(T):
                    dve.wait_ge(w_steps, ST_G * group + K + t)
                    if group == 1:
                        V.tensor_copy(natv[:, t, 256:NV], PS[:, t, 0:272]).then_inc(acc_free, 1)
                    else:
                        V.tensor_copy(nat[:, t, NA - 256:NA], PS[:, t, 0:256])
                        V.tensor_copy(natv[:, t, 0:256], PS[:, t, 256:512]).then_inc(acc_free, 1)

            dve.wait_ge(vec_landed, 16 * 5)
            V.tensor_copy(posf[:, :], posi[:, :]).then_inc(vec_ready, 1)
            dve.wait_ge(x_squared, 2)
            link(mean_square(0, 2, 1.0 / D))
            rsqrt(0, 2)
            normed(X0, 0, 0, [0])
            dve.wait_ge(vec_T, 1)
            V.tensor_copy(vT[:, :], PS[:, 0, 0:19])
            V.tensor_copy(pT[:, :], PS[:, 0, 32:32 + T]).then_inc(vec_ready, 1)
            normed(X0, 0, 0, [1])
            dve.wait_ge(vec_ready, 2)
            for k in range(K // 2):
                gained_lo(hT_h, hT_l, 0, 0, k)
            dve.wait_ge(x_squared, T)
            link(mean_square(2, T, 1.0 / D))
            rsqrt(2, T)
            for c in range(2):
                for k in (K // 2 + 2 * c, K // 2 + 2 * c + 1):
                    gained_lo(hT_h, hT_l, 0, 0, k)
                normed(X0, 0, 1, [c])
            for k in range(K):
                gained_lo(hT_h, hT_l, 0, 1, k)

            dve.wait_ge(consts, 6)
            half = HD // 2
            a0 = ang[:, 2, :, :]
            link(V.tensor_tensor(a0, pT[:, :].unsqueeze(2).to_broadcast([P, T, half]),
                                 invf[:, :].unsqueeze(1).to_broadcast([P, T, half]), ALU.mult))
            magic = 1.5 * 2.0 ** 23
            two_pi = 2.0 * np.pi
            c1 = 6.28125
            c2 = float(np.float32(np.round((two_pi - c1) * 2 ** 22) / 2 ** 22))
            c3 = float(np.float32(two_pi - c1 - c2))
            for n, (turn, shift) in enumerate(((0.25, np.pi / 2), (0.0, 0.0))):
                r, q = ang[:, n, :, :], ang[:, 3 + n, :, :]
                link(V.tensor_scalar(q, a0, 1.0 / two_pi, turn, ALU.mult, ALU.add))
                link(V.tensor_scalar(q, q, magic, None, ALU.add))
                link(V.tensor_scalar(q, q, magic, None, ALU.subtract))
                link(V.scalar_tensor_tensor(r, q, -c1, a0, ALU.mult, ALU.add))
                link(V.scalar_tensor_tensor(r, q, -c2, r, ALU.mult, ALU.add))
                link(V.scalar_tensor_tensor(r, q, -c3, r, ALU.mult, ALU.add))
                link(V.tensor_scalar(r, r, float(shift), 3.1415925, ALU.add, ALU.min))
                last = V.tensor_scalar(r, r, -3.1415925, None, ALU.max)
                last.then_inc(ang_ready, 1) if n else link(last)

            for j in range(4):
                dve.wait_ge(w_steps, K + j)
                V.tensor_scalar(qk[:, j, :], PS[:, j, :], GDK ** -0.5 if j < 2 else 1.0, None,
                                ALU.mult).then_inc(acc_free, 1)

            dve.wait_ge(small_landed, 16 * 6)
            V.tensor_scalar(nsinks[:, :], sinks[:, :], -1.0, None, ALU.mult)
            V.tensor_scalar(gain[:, 0, :], gain[:, 0, :], HD ** -0.5, None, ALU.mult)
            link(V.tensor_scalar(gain[:, 2, :], gain[:, 2, :], HD ** -0.5, None, ALU.mult))
            dve.wait_ge(sin_done, 2)
            for n in range(4):
                g1 = gain[:, n, 0:half].unsqueeze(1).to_broadcast([P, T, half])
                g2 = gain[:, n, half:HD].unsqueeze(1).to_broadcast([P, T, half])
                V.tensor_tensor(ctab[:, n, :, 0:half], ang[:, 0, :, :], g1, ALU.mult)
                V.tensor_tensor(ctab[:, n, :, half:HD], ang[:, 0, :, :], g2, ALU.mult)
                V.tensor_tensor(stab[:, n, :, 0:half], ang[:, 1, :, :], g1, ALU.mult)
                link(V.tensor_tensor(stab[:, n, :, half:HD], ang[:, 1, :, :], g2, ALU.mult))
                link(V.tensor_scalar(stab[:, n, :, half:HD], stab[:, n, :, half:HD], -1.0, None, ALU.mult))
            evacuate(1)
            dve.wait_ge(low_T, 1)
            V.tensor_copy(alT[:, :], PS[0:RANK, 4, :]).then_inc(low_ready, 1)
            for p in range(2):
                dve.wait_ge(z_done, p + 1)
                V.tensor_scalar(lab[:, p, :], PS[:, 5 + p, :], vT[:, 16 + p:17 + p], 0.0,
                                ALU.add, ALU.min).then_inc(z_read, 1)
            for p in range(2):
                dve.wait_ge(soft_done, p + 1)
                if p == 0:
                    dve.wait_ge(z_read, 2)
                link(V.tensor_tensor(lab[:, p, :], lab[:, p, :], gx[:, p, :], ALU.subtract))
                V.tensor_tensor_scan(lab[:, p, :], once[:, :], lab[:, p, :], 0.0,
                                     ALU.mult, ALU.add).then_inc(b_ready, 1)
            for p in range(2):
                if p == 0:
                    dve.wait_ge(b_ready, 2)
                b3 = lab[:, p, :].rearrange("p (c t) -> p c t", t=GC)
                V.tensor_tensor(kt[:, p, :].rearrange("p (c t) -> p c t", t=GC),
                                b3[:, :, GC - 1:GC].to_broadcast([P, NCH, GC]), b3,
                                ALU.subtract).then_inc(b_ready, 1)
            for p in range(2):
                dve.wait_ge(gexp, 2 * p + 1)
                V.tensor_tensor(qk[:, p, :], qk[:, p, :], gx[:, p, :], ALU.mult).then_inc(gexp_used, 1)
            evacuate(2)
            for p in range(2):
                dve.wait_ge(gexp, 5 + p)
                V.tensor_tensor(kt[:, p, :], qk[:, 2 + p, :], gx[:, p, :], ALU.mult).then_inc(gexp_used, 1)
            for p in range(2):
                dve.wait_ge(gexp, 7 + p)
                V.tensor_tensor(qk[:, 2 + p, :], qk[:, 2 + p, :], gx[:, p, :], ALU.mult).then_inc(gexp_used, 1)

            for n in range(2):
                dve.wait_ge(kt_T, n + 1)
                V.tensor_copy(ktn[:, 2 * n:2 * n + 2, :], PS[:, 4 + n, :]
                              .rearrange("p (t n) -> p t n", t=2)).then_inc(kt_ready, 1)

            def masked(tt):
                for hh in range(2):
                    dve.wait_ge(a_done, 2 * tt + hh + 1)
                    for t in range(2):
                        src = PS[:, 6 + hh, t * 256:(t + 1) * 256].rearrange("p (a n) -> p a n", a=2)
                        last = V.copy_predicated(am[:, 2 * tt + t, hh, :, :],
                                                 cmask[:, :].unsqueeze(1).to_broadcast([P, 2, P]), src)
                    last.then_inc(a_ready, 1)

            dve.wait_ge(am_zero, 2)
            masked(0)
            masked(1)

            def states(p):
                for c in range(NCH - 1):
                    dve.wait_ge(ds_done, 2 * p + c % 2 + 1)
                    last = V.scalar_tensor_tensor(st[:, p, c + 1, :], st[:, p, c, :], dec[:, p, c:c + 1],
                                                  PS[:, 4 + c % 2, (c // 2) * P:(c // 2 + 1) * P],
                                                  ALU.mult, ALU.add)
                    last.then_inc(st_ready, 1) if c == NCH - 2 else link(last)

            states(0)
            states(1)

            def rope(n):
                dve.wait_ge(rope_sq, n + 1)
                parts, h0 = [], 0
                for c0, heads, table in CHUNKS[n]:
                    parts.append((h0, c0, heads, table))
                    last = V.reduce_sum(ss[:, T * h0:T * (h0 + heads)].rearrange("p (t h) -> p t h", h=heads),
                                        sqr[:, :, h0:h0 + heads, :], AX_X)
                    h0 += heads
                last.then_inc(sqr_read, 1)
                dve.wait_ge(sqr_read, n + 1)
                link(mean_square(0, T * h0, 1.0 / HD))
                rsqrt(0, T * h0)

                def view(h0, c0, heads, table):
                    xs = nat[:, :, c0:c0 + heads * HD].rearrange("p t (h d) -> p t h d", d=HD)
                    return (xs, [P, T, heads, HD], ropa[:, :, h0:h0 + heads, :], ropb[:, :, h0:h0 + heads, :],
                            ry[:, T * h0:T * (h0 + heads)].rearrange("p (t h) -> p t h", h=heads))

                for part in parts:
                    xs, full, a, b, rs = view(*part)
                    last = V.tensor_tensor(xs, xs, rs.unsqueeze(3).to_broadcast(full), ALU.mult)
                link(last)
                for part in parts:
                    xs, full, a, b, rs = view(*part)
                    V.tensor_tensor(a, xs, ctab[:, part[3], :, :].unsqueeze(2).to_broadcast(full), ALU.mult)
                    last = V.tensor_tensor(b, xs, stab[:, part[3], :, :].unsqueeze(2).to_broadcast(full),
                                           ALU.mult)
                link(last)
                for part in parts:
                    xs, full, a, b, rs = view(*part)
                    V.tensor_tensor(xs[:, :, :, 0:half], a[:, :, :, 0:half], b[:, :, :, half:HD], ALU.add)
                    last = V.tensor_tensor(xs[:, :, :, half:HD], a[:, :, :, half:HD], b[:, :, :, 0:half],
                                           ALU.add)
                last.then_inc(rope_done, 1)

            rope(0)
            for t in range(T):
                dve.wait_ge(o_squared, t + 1)
                last = V.reduce_sum(ss[:, t * GH:(t + 1) * GH],
                                    osq[:, t, :].rearrange("p (h v) -> p h v", v=GDV), AX_X)
            link(last)
            link(mean_square(0, T * GH, 1.0 / GDV))
            rsqrt(0, T * GH)
            dve.wait_ge(o_copied, T)
            o4 = natv[:, :, 0:BW].rearrange("p t (h v) -> p t h v", v=GDV)
            V.tensor_tensor(o4, o4, ry[:, 0:T * GH].rearrange("p (t h) -> p t h", h=GH).unsqueeze(3)
                            .to_broadcast([P, T, GH, GDV]), ALU.mult).then_inc(o_normed, 1)
            link(V.tensor_scalar(vT[:, 18:19], vT[:, 18:19], 0.5, None, ALU.mult))
            rope(1)
            rope(2)
            rope(3)

            def output_gate(i):
                j = R_ORDER[i]
                dve.wait_ge(r_tanh, i + 1)
                V.scalar_tensor_tensor(srT[:, j, :], srT[:, j, :], 1.0, PS[:, j, :],
                                       ALU.add, ALU.mult).then_inc(acc_free, 1)

            def gated(j):
                V.scalar_tensor_tensor(ycT[:, j, :], PS[:, 4 + j, :], vT[:, 18:19], srT[:, j, :],
                                       ALU.mult, ALU.mult).then_inc(yc_done, 1)

            output_gate(0)
            output_gate(1)
            dve.wait_ge(yc_T, BR)
            dve.wait_ge(acc_free, 29)
            gated(0)
            output_gate(2)
            output_gate(3)
            dve.wait_ge(acc_free, 32)
            for j in range(1, BR):
                gated(j)

            before, LINKS = seq[1], 3
            with dve.Fori(0, KV) as g:
                with dve.Fori(0, GPK) as m:
                    h = g * GPK + m
                    seq[0], seq[1] = h * LINKS, before
                    for n in range(2):
                        dve.wait_ge(qkT_hi, h * 2 + (n + 1))
                        V.tensor_tensor(qkT_l[:, n, :], PS[:, 3 + n, :], qkT_h[:, n, :].bitcast(F32),
                                        ALU.subtract).then_inc(qkT_ready, 1)

                    def top(col, bank, c0, w, count=1):
                        src = PS[:, bank, c0:c0 + w * count]
                        if count > 1:
                            src = src.rearrange("p (a n) -> p a n", a=count)
                        return V.reduce_max(mx[:, col:col + count], src, AX_X, negate=True)

                    dve.wait_ge(scores, h * 5 + 1)
                    top(2, 4, 0, 384)
                    dve.wait_ge(scores, h * 5 + 2)
                    top(1, 5, 0, 256)
                    top(0, 5, 256, 128)
                    dve.wait_ge(scores, h * 5 + 3)
                    top(3, 3, 0, 512).then_inc(negmax, 1)
                    dve.wait_ge(scores, h * 5 + 4)
                    top(5, 6, 0, 256, 2)
                    dve.wait_ge(scores, h * 5 + 5)
                    top(7, 7, 0, 256)
                    link(top(4, 7, 256, 128))
                    V.tensor_scalar(mx[:, 4:8], mx[:, 4:8], nsinks[:, bass.ds(h, 1)], None,
                                    ALU.min).then_inc(negmax, 1)
                    dve.wait_ge(probs, h * 9 + 9)
                    link(V.tensor_tensor(den[:, 4:8], den[:, 4:8], esk[:, :], ALU.add))
                    link(V.reciprocal(rec[:, :], den[:, :]))
                    for bank in (3, 5, 7):
                        dve.wait_ge(pr_T, h * 5 + (bank - 2))
                        n = 4 * (bank - 3)
                        w = min(4, NPR - n)
                        V.tensor_copy(prT[:, n:n + w, :], PS[:, bank, 0:w * P]
                                      .rearrange("p (a n) -> p a n", n=P)).then_inc(prT_v, 1)
                    dve.wait_ge(pv, h + 1)
                    for n, c0 in enumerate((C_QB, C_QA)):
                        V.tensor_tensor(nat[:, :, bass.ds(h * HD + c0, HD)],
                                        PS[:, 2, n * 256:(n + 1) * 256].rearrange("p (t d) -> p t d", d=HD),
                                        rec[:, 4 * n:4 * n + 4].unsqueeze(2).to_broadcast([P, T, HD]),
                                        ALU.mult).then_inc(y_ready, 1)
                    assert seq[1] - before == LINKS
            seq[0], seq[1] = 0, before + HEADS * LINKS

            for i, n in enumerate(Y_ORDER):
                dve.wait_ge(y_hi, BR + i + 1 if i else 1)
                V.tensor_tensor(ya_l[:, n, :], PS[:, Y_BANK[i], :], ya_h[:, n, :].bitcast(F32),
                                ALU.subtract).then_inc(y_lo, 1)
                if i == 0:
                    for b in range(2):
                        dve.wait_ge(y_hi, b + 2)
                        V.tensor_tensor(yc_l[:, b, :], ycT[:, b, :], yc_h[:, b, :].bitcast(F32),
                                        ALU.subtract).then_inc(y_lo, 1)

            before, LINKS = seq[1], 4
            with dve.Fori(0, 4) as j:
                seq[0], seq[1] = j * LINKS, before
                for u in range(2):
                    for i, b in enumerate(B_ORDER):
                        dve.wait_ge(w_steps, j * ST_BR + (ST_BR0 + 6 * u + (i + 1 if i < 2 else 6)))
                        last = V.scalar_tensor_tensor(mtmp[:, i, :], tg[:, bass.ds(j * 2 + u, 1), b, :], 1.0,
                                                      PS[:, 3 * u + b, :], ALU.add, ALU.mult)
                        if i == 1:
                            link(last)
                            link(V.tensor_tensor(mtmp[:, 0, :], mtmp[:, 0, :], mtmp[:, 1, :], ALU.add))
                    last.then_inc(merge_read, 1)
                    dve.wait_ge(merge_read, j * 2 + (u + 3))
                    V.tensor_tensor(mtmp[:, 3, :], mtmp[:, 0, :], mtmp[:, 2, :], ALU.add).then_inc(merged, 1)
                    dve.wait_ge(m_hi, j * 2 + (u + 1))
                    V.scalar_tensor_tensor(mT_l[:, bass.ds(j * 2 + u, 1), :], mtmp[:, 3, :], 0.5,
                                           mT_h[:, bass.ds(j * 2 + u, 1), :].bitcast(F32),
                                           ALU.mult, ALU.subtract).then_inc(m_lo, 1)
                assert seq[1] - before == LINKS
            seq[0], seq[1] = 0, before + 4 * LINKS

            dve.wait_ge(x_again, 16 * T)
            def residual(c, t, step):
                dve.wait_ge(w_steps, ST_O0 + ST_G * c + step)
                V.tensor_tensor(X[:, t, c * 512:(c + 1) * 512], X[:, t, c * 512:(c + 1) * 512],
                                PS[:, t, :], ALU.add).then_inc(acc_free, 1)

            for t in range(T):
                residual(0, t, K + t)
            dve.wait_ge(x_squared, 2 * T)
            link(mean_square(0, T, 1.0 / D))
            def second_half(t0):
                dve.wait_ge(x_squared, 2 * T + t0 + 2)
                link(V.scalar_tensor_tensor(rv[:, t0:t0 + 2], ss[:, T + t0:T + t0 + 2], FACTOR / D,
                                            rv[:, t0:t0 + 2], ALU.mult, ALU.add))
                rsqrt(t0, t0 + 2)

            residual(1, 0, 1)
            residual(1, 1, 2)
            second_half(0)
            normed(X, 1, 0)
            residual(1, 2, 3)
            for k in range(K):
                gained_lo(fT_h, fT_l, 1, 0, k)
            residual(1, 3, ST_G)
            second_half(2)
            normed(X, 1, 1)
            for k in range(K):
                gained_lo(fT_h, fT_l, 1, 1, k)

            def swiglu(c, u):
                step = c * ST_G + ST_F0
                for f in range(2):
                    dve.wait_ge(f_tanh, c * 2 + (f + 1))
                    V.scalar_tensor_tensor(fa[:, 2 + f, :], fa[:, f, :], 1.0, PS[:, 4 * u + f, :],
                                           ALU.add, ALU.mult).then_inc(f_mid, 1)
                    dve.wait_ge(f_mid, c * 2 + (f + 1))
                    dve.wait_ge(w_steps, step + (K + 2 * f + 1))
                    V.scalar_tensor_tensor(fa[:, 4 + f, :], fa[:, 2 + f, :], 0.5, PS[:, 4 * u + 2 + f, :],
                                           ALU.mult, ALU.mult).then_inc(f_read, 1)
                for f in range(2):
                    dve.wait_ge(f_hi, c * 2 + (f + 1))
                    V.tensor_tensor(aT_l[:, bass.ds(c * 2 + f, 1), :], fa[:, 4 + f, :],
                                    aT_h[:, bass.ds(c * 2 + f, 1), :].bitcast(F32),
                                    ALU.subtract).then_inc(f_lo, 1)

            with dve.Fori(0, FG // 2) as j:
                for u in range(2):
                    swiglu(j * 2 + u, u)
            swiglu(FG - 1, 0)

            with dve.Fori(0, 2) as c:
                for t in range(T):
                    dve.wait_ge(w_steps, c * ST_D + (ST_D0 + FK + t))
                    part = X[:, t, bass.ds(c * 512, 512)]
                    V.tensor_tensor(part, part, PS[:, 4 + t, :], ALU.add).then_inc(y_out, 1)

        @block.tensor
        def _(pe):
            mm = nc.tensor.matmul

            def three(dst, st_h, st_l, mv_h, mv_l, start, stop):
                mm(dst, st_h, mv_h, start=start, stop=False)
                mm(dst, st_h, mv_l, start=False, stop=False)
                return mm(dst, st_l, mv_h, start=False, stop=stop)

            def four_bank_group(g, free, feature_major, a_h, a_l, width=512, inside=None, banks=0,
                                order=range(4), inputs=None, bank_3_free=None, tokens=slice(0, S), last_use=True):
                for k in range(K):
                    pe.wait_ge(lo_done, g * K + (k + 1))
                    if inputs:
                        inputs(k)
                    for n in order:
                        if k == 0 and free is not None:
                            pe.wait_ge(acc_free, free + (n + 1))
                        if k == 0 and n == 3 and bank_3_free:
                            bank_3_free()
                        if feature_major:
                            w = slice(n * P, (n + 1) * P)
                            last = three(PS[:, banks + n, tokens], whi[k][:, w], wlo[k][:, w],
                                         a_h[:, k, tokens], a_l[:, k, tokens], k == 0, k == K - 1)
                        else:
                            tok = slice(n * P, (n + 1) * P)
                            last = three(PS[:, banks + n, 0:width], a_h[:, k, tok], a_l[:, k, tok],
                                         whi[k][:, 0:width], wlo[k][:, 0:width], k == 0, k == K - 1)
                        if k == K - 1 and last_use:
                            last.then_inc(w_steps, 1)
                    if k < K - 1 and last_use:
                        last.then_inc(w_steps, 1)
                    if inside and k in inside:
                        inside[k]()

            def normed_T(norm, half, i):
                if i in (0, 2):
                    pe.wait_ge(xn_ready, 4 * norm + 2 * half + i // 2 + 1)
                if half:
                    pe.wait_ge(hT_done, 16 * norm + 2 * i + 2)
                for kk in range(2):
                    for tt in range(2):
                        c = kk * 256 + tt * P
                        last = nc.tensor.transpose(PS[:, 4 + i, c:c + P],
                                                   xn[:, tt, (2 * i + kk) * P:(2 * i + kk + 1) * P], ident[:, :])
                last.then_inc(x_T, 1)

            def first_group(norm, g, free, h_h, h_l, order):
                for half in range(2):
                    four_bank_group(g, None if half else free, True, h_h, h_l, order=order,
                                    inputs=lambda k: pe.wait_ge(hT_done, 16 * norm + 8 * half + k + 1),
                                    inside=None if half else {4 + i: (lambda i=i: normed_T(norm, 1, i))
                                                              for i in range(4)},
                                    tokens=slice(half * 256, (half + 1) * 256), last_use=half == 1)

            pe.wait_ge(consts, 2)

            def keep_warm(products):
                for _ in range(products):
                    mm(PS[:, 1, 0:P], ident[:, :], ident[:, :], start=True, stop=True)

            keep_warm(WARM[0])
            pe.wait_ge(vec_ready, 1)
            pe.wait_ge(vec_landed, 16 * 5)
            nc.tensor.transpose(PS[:, 0, 0:19], vecs[:, :], ident[0:19, 0:19])
            nc.tensor.transpose(PS[:, 0, 32:32 + T], posf[:, :], ident[0:T, 0:T]).then_inc(vec_T, 1)
            keep_warm(WARM[1])
            for i in range(4):
                normed_T(0, 0, i)
            first_group(0, 0, None, hT_h, hT_l, range(4))

            def low_transposes():
                pe.wait_ge(acc_free, 8)
                for t in range(T):
                    last = nc.tensor.transpose(PS[0:RANK, 4, t * P:(t + 1) * P],
                                               natv[:, t, LOW:NV], ident[:, :])
                last.then_inc(low_T, 1)

            def decay_logits():
                pe.wait_ge(low_ready, 1)
                for p in range(2):
                    mm(PS[:, 5 + p, :], wal[:, p * P:(p + 1) * P], alT[:, :],
                       start=True, stop=True).then_inc(z_done, 1)

            def a_products(tt):
                for hh in range(2):
                    r = slice(hh * GDK, (hh + 1) * GDK)
                    for t in range(2):
                        tok = slice((2 * tt + t) * P, (2 * tt + t + 1) * P)
                        for p in range(2):
                            c = (2 * t + p) * P
                            last = mm(PS[:, 6 + hh, c:c + P], qk[r, 2 + p, tok], qk[r, p, tok],
                                      start=True, stop=True)
                    last.then_inc(a_done, 1)

            def tails_and_a():
                pe.wait_ge(gexp_used, 6)
                pe.wait_ge(z_read, 2)
                for n in range(2):
                    for t in range(2):
                        for p in range(2):
                            last = nc.tensor.transpose(PS[:, 4 + n, (2 * t + p) * P:(2 * t + p + 1) * P],
                                                       kt[:, p, (2 * n + t) * P:(2 * n + t + 1) * P],
                                                       ident[:, :])
                    last.then_inc(kt_T, 1)
                a_products(0)

            def state_updates(p):
                if p:
                    pe.wait_ge(st_ready, p)
                for par in range(2):
                    r = slice(par * GC, (par + 1) * GC)
                    for t in range(T):
                        for hh in range(2):
                            h = 2 * p + hh
                            last = mm(PS[hh * GDK:(hh + 1) * GDK, 4 + par, t * P:(t + 1) * P],
                                      ktn[r, t, h * GDK:(h + 1) * GDK], natv[r, t, h * GDV:(h + 1) * GDV],
                                      start=True, stop=True)
                    last.then_inc(ds_done, 1)

            def a_and_states():
                pe.wait_ge(kt_ready, 2)
                state_updates(0)
                pe.wait_ge(a_ready, 2)
                a_products(1)

            def outputs():
                pe.wait_ge(a_ready, 4)
                pe.wait_ge(st_ready, 2)
                for hh in range(2):
                    r = slice(hh * GDK, (hh + 1) * GDK)
                    for t in range(T):
                        if hh:
                            pe.wait_ge(o_half, t + 1)
                        for p in range(2):
                            h = 2 * p + hh
                            v = slice(h * GDV, (h + 1) * GDV)
                            mm(PS[:, 4 + t, v], am[:, t, hh, p, :], natv[:, t, v], start=True, stop=False,
                               skip_group_check=True)
                            for ch in range(2):
                                tok = slice(t * P + ch * GC, t * P + (ch + 1) * GC)
                                last = mm(PS[ch * GC:(ch + 1) * GC, 4 + t, v], qk[r, p, tok],
                                          st[r, p, 2 * t + ch, :], start=False, stop=True,
                                          skip_group_check=True)
                        last.then_inc(o_done if hh else o_half, 1)

            def token_group(g, **kw):
                four_bank_group(g, 4 * (g - 1), False, hT_h, hT_l, **kw)

            def gla_transposes():
                pe.wait_ge(o_normed, 1)
                for j in range(BR):
                    for t in range(T):
                        last = nc.tensor.transpose(PS[:, 4 + j, t * P:(t + 1) * P],
                                                   natv[:, t, j * P:(j + 1) * P], ident[:, :])
                    last.then_inc(yc_T, 1)

            token_group(1, width=272)
            token_group(2, inside={1: low_transposes, 2: decay_logits})
            token_group(3, inside={3: tails_and_a, 6: a_and_states})
            token_group(4, inside={1: lambda: state_updates(1), 4: outputs})
            token_group(5)
            token_group(6, inside={1: gla_transposes})
            four_bank_group(7, 4 * 6, True, hT_h, hT_l, order=R_ORDER)

            with pe.Fori(0, KV) as g:
                with pe.Fori(0, GPK) as m:
                    h = g * GPK + m

                    def qk_transposes():
                        pe.wait_ge(acc_free, 30)
                        pe.wait_ge(yc_done, 1)
                        for n in range(2):
                            if n:
                                pe.wait_ge(kstaged, g + 1)
                            pe.wait_ge(staged, h * 3 + (2 + n))
                            for t in range(T):
                                last = nc.tensor.transpose(PS[:, 3 + n, t * P:(t + 1) * P],
                                                           stg[:, t, n, :, :], ident[:, :])
                            last.then_inc(qk_T, 1)

                    def gate_tile(b, bank):
                        for k in range(K):
                            if b == 0 and k == K // 2:
                                qk_transposes()
                            if b == 0:
                                pe.wait_ge(lo_done, h * K + (8 * K + k + 1))
                            w = slice(b * P, (b + 1) * P)
                            last = three(PS[:, bank, :], whi[k][:, w], wlo[k][:, w],
                                         hT_h[:, k, :], hT_l[:, k, :], k == 0, k == K - 1)
                            if b == 2 or k == K - 1:
                                last.then_inc(w_steps, 1)

                    pe.wait_ge(acc_free, 29)
                    pe.wait_ge(gate_read, h * 3 + 1)
                    gate_tile(0, 0)

                    pe.wait_ge(yc_done, BR)
                    pe.wait_ge(acc_free, 32)
                    pe.wait_ge(qkT_ready, h * 2 + 2)

                    def score_tile(at, r, t, k0, w, mask):
                        bank, col = at
                        wide = slice(k0, k0 + max(w, 2 * P))
                        q_h, q_l = qkT_h[r, 0, t * P:(t + 1) * P], qkT_l[r, 0, t * P:(t + 1) * P]
                        three(PS[:, bank, col:col + max(w, 2 * P)], q_h, q_l,
                              qkT_h[r, 1, wide], qkT_l[r, 1, wide], True, False)
                        return mm(PS[:, bank, col + w - mask:col + w], identb[:, :], wmask[:, 2 * P - mask:],
                                  start=False, stop=True)

                    def moba_scores(t):
                        return score_tile(M_AT[t], slice(HD, P), t, 0, (t + 1) * P, P)

                    def window_scores(t):
                        w = P if t == 0 else 2 * P
                        return score_tile(S_AT[t], slice(0, HD), t, (t + 1) * P - w, w, w)

                    moba_scores(2).then_inc(scores, 1)
                    moba_scores(1)
                    moba_scores(0).then_inc(scores, 1)
                    moba_scores(3).then_inc(scores, 1)
                    window_scores(1)
                    window_scores(2).then_inc(scores, 1)
                    window_scores(3)
                    window_scores(0).then_inc(scores, 1)

                    gate_tile(1, 1)
                    pe.wait_ge(probs, h * 9 + 8)
                    for n in range(NPR):
                        last = nc.tensor.transpose(PS[:, 3 + n // 4, (n % 4) * P:(n % 4 + 1) * P],
                                                   pr[:, n * P:(n + 1) * P], ident[:, :])
                        if n % 4 == 3 or n == NPR - 1:
                            last.then_inc(pr_T, 1)
                    pe.wait_ge(gate_read, h * 3 + 2)
                    gate_tile(2, 0)
                    pe.wait_ge(prT_v, h * 3 + 3)
                    pe.wait_ge(prT_a, h * 2 + 2)
                    pe.wait_ge(y_ready, h * 2 + 1)
                    for n, (first, v0, lo) in enumerate(
                            ((M_PR, h * HD + C_VB, lambda t: 0), (S_PR, g * HD + C_VA, lambda t: max(0, t - 1)))):
                        for t in range(T):
                            for kk in range(lo(t), t + 1):
                                last = mm(PS[:, 2, n * 256 + t * HD:n * 256 + (t + 1) * HD],
                                          prT[:, first[t] + kk - lo(t), :], nat[:, kk, bass.ds(v0, HD)],
                                          start=kk == lo(t), stop=kk == t)
                    last.then_inc(pv, 1)

            for i, n in enumerate(Y_ORDER):
                if Y_BANK[i] == 0:
                    pe.wait_ge(gate_read, 3 * HEADS + 1)
                if n in (BR - 1, 2 * BR - 1):
                    pe.wait_ge(y_ready, 2 * HEADS + 1)
                if i == 2 * BR - 1:
                    pe.wait_ge(y_lo, 1)
                c0 = n * P if n < BR else C_QB + (n - BR) * P
                for t in range(T):
                    last = nc.tensor.transpose(PS[:, Y_BANK[i], t * P:(t + 1) * P], nat[:, t, c0:c0 + P],
                                               ident[:, :])
                last.then_inc(y_T, 1)

            with pe.Fori(0, 4) as j:
                for u in range(2):
                    pe.wait_ge(merge_read, j * 2 + (u + 1))
                    for i, b in enumerate(B_ORDER):
                        for k in range(BR):
                            s = BR * u + k
                            if i == 0:
                                pe.wait_ge(lo_done, j * K + (16 * K + s + 1))
                            if u == 0 and i < 2:
                                if i == 0 and k >= 2:
                                    pe.wait_ge(yc_lo, k - 1)
                                else:
                                    pe.wait_ge(y_lo, k + 2 if i == 0 else 2 + (2 * BR if k == BR - 1 else 5))
                            w = slice(b * P, (b + 1) * P)
                            y_h, y_l, n = (ya_h, ya_l, BR * b + k) if b < 2 else (yc_h, yc_l, k)
                            last = three(PS[:, 3 * u + b, :], whi[s][:, w], wlo[s][:, w],
                                         y_h[:, n, :], y_l[:, n, :], k == 0, k == BR - 1)
                            if i == 2 or k == BR - 1:
                                last.then_inc(w_steps, 1)

            pe.wait_ge(merge_read, 2 + K - 1)

            four_bank_group(20, 4 * 7, False, mT_h, mT_l, inputs=lambda k: pe.wait_ge(m_lo, k + 1),
                            bank_3_free=lambda: pe.wait_ge(merge_read, 2 + K))
            for t in range(T):
                pe.wait_ge(acc_free, 4 * 8 + t + 1)
                if t == T - 1:
                    for i in range(4):
                        normed_T(1, 0, i)
                for k in range(K):
                    if t == 0:
                        pe.wait_ge(lo_done, 21 * K + k + 1)
                    tok = slice(t * P, (t + 1) * P)
                    last = three(PS[:, t, :], mT_h[:, k, tok], mT_l[:, k, tok], whi[k][:, :], wlo[k][:, :],
                                 k == 0, k == K - 1)
                    if t == T - 1 or k == K - 1:
                        last.then_inc(w_steps, 1)

            first_group(1, 22, 4 * 9, fT_h, fT_l, (0, 2, 1, 3))

            def swiglu(c, u):
                pe.wait_ge(f_read, c * 2 + 1)
                four_bank_group(c + 22, None, True, fT_h, fT_l, banks=4 * u, order=(0, 2, 1, 3))

            with pe.Fori(0, FG // 2) as j:
                for u in range(2):
                    swiglu(j * 2 + (u + 1), 1 - u)

            pe.wait_ge(f_read, 3 + 2 * (FG - 1))
            with pe.Fori(0, 2) as c:
                for k in range(FK):
                    s = k % DRING
                    pe.wait_ge(lo_done, c * FK + (K * (22 + FG) + k + 1))
                    if k in (0, FK - 2, FK - 1):
                        pe.wait_ge(f_lo, k + 1 if k else FK - 2)
                    for t in range(T):
                        if k == 0:
                            pe.wait_ge(y_out, c * T + (t + 1))
                        tok = slice(t * P, (t + 1) * P)
                        last = three(PS[:, 4 + t, :], aT_h[:, k, tok], aT_l[:, k, tok], whi[s][:, :], wlo[s][:, :],
                                     k == 0, k == FK - 1)
                        if k == FK - 1:
                            last.then_inc(w_steps, 1)
                    if k < FK - 1:
                        last.then_inc(w_steps, 1)


_OUT_SHAPE = (1, S, D)
_INS = ["x", "positions", "attn_norm", "w_in", "swa_q_norm", "swa_k_norm", "swa_sinks", "moba_q_norm",
        "moba_k_norm", "gla_w_alpha", "gla_b_alpha", "gla_out_norm", "w_branch_swa", "w_branch_moba",
        "w_branch_gla", "w_out", "ffn_norm", "w_ffn_gate", "w_ffn_up", "w_ffn_down"]
_PLAIN = {"w_in", "w_branch_swa", "w_branch_moba", "w_branch_gla", "w_out", "w_ffn_gate", "w_ffn_up",
          "w_ffn_down"}


def kernel(**inputs):
    import concourse.bacc as bacc
    from concourse.bass_utils import run_bass_kernel_spmd

    nc = bacc.Bacc("TRN2", target_bir_lowering=False, num_devices=1)
    arrays, args = {}, []
    for name in _INS:
        a = np.ascontiguousarray(inputs[name])
        if name in _PLAIN:
            a = a[0]
        arrays[f"in_{name}"] = a
        args.append(nc.dram_tensor(f"in_{name}", a.shape, mybir.dt.from_np(a.dtype), kind="ExternalInput").ap())
    args.append(nc.dram_tensor("out", _OUT_SHAPE, F32, kind="ExternalOutput").ap())
    build_layer(nc, *args)
    r = run_bass_kernel_spmd(nc, [arrays], core_ids=[0])
    return r.results[0]["out"]
```
